# Optimizing a Trainium2 kernel written in Bass

```python
import jax, jax.numpy as jnp
from jax import lax
import numpy as np

D_MODEL = 1024
BATCH = 1
SEQ = 512
DEPTH = 2

GRID_W = 64
CTX_LEN = 256
N_MIXERS = 2
N_ATTN_LAYERS = (DEPTH + N_MIXERS - 1) // N_MIXERS
N_GLA_LAYERS = DEPTH // N_MIXERS
RMS_EPS = 1e-6
ATTN_HEAD_DIM = 64
ATTN_HEADS = D_MODEL // ATTN_HEAD_DIM
ATTN_KV_HEADS = 4
ATTN_GROUP = ATTN_HEADS // ATTN_KV_HEADS
WINDOW = 128
ATTN_BLOCK = 128
ATTN_HALO = -(-WINDOW // ATTN_BLOCK) * ATTN_BLOCK
ROPE_THETA = 10000.0
ROPE_AXIS_DIM = ATTN_HEAD_DIM // 2
GLA_HEADS = 4
GLA_KEY_DIM = D_MODEL // 2 // GLA_HEADS
GLA_VAL_DIM = D_MODEL // GLA_HEADS
GLA_GATE_RANK = 16
GLA_GATE_NORM = 16.0
GLA_CHUNK = 64
N_EXPERTS = 16
N_GROUPS = 4
EXPERTS_PER_GROUP = N_EXPERTS // N_GROUPS
TOP_K = 2
D_EXPERT = D_MODEL // 2
MOE_BLOCK = 256

kernel_name = 'hybrid_swa_gla_grouped_moe_dit'

F32 = jnp.float32

def rmsnorm(x, gain):
    xf = x.astype(F32)
    y = xf * lax.rsqrt(jnp.mean(xf * xf, axis=-1, keepdims=True) + RMS_EPS) * gain.astype(F32)
    return y.astype(x.dtype)

def modulate(h, shift, scale):
    return h * (1 + scale) + shift

def axial_rope_tables(rows):
    row = jnp.repeat(jnp.arange(rows, dtype=F32), GRID_W)
    col = jnp.tile(jnp.arange(GRID_W, dtype=F32), rows)
    half = ROPE_AXIS_DIM // 2
    inv_freq = ROPE_THETA ** (-jnp.arange(half, dtype=F32) / half)
    ang_r = row[:, None] * inv_freq[None, :]
    ang_c = col[:, None] * inv_freq[None, :]
    return (jnp.cos(ang_r), jnp.sin(ang_r), jnp.cos(ang_c), jnp.sin(ang_c))

def rope_2d(x, rope):
    cos_r, sin_r, cos_c, sin_c = rope
    shp = (x.shape[1],) + (1,) * (x.ndim - 3) + (ROPE_AXIS_DIM // 2,)
    xf = x.astype(F32)

    def rot(y, cos, sin):
        y1, y2 = jnp.split(y, 2, axis=-1)
        cos, sin = cos.reshape(shp), sin.reshape(shp)
        return jnp.concatenate([y1 * cos - y2 * sin, y2 * cos + y1 * sin], axis=-1)

    x_row, x_col = jnp.split(xf, 2, axis=-1)
    return jnp.concatenate([rot(x_row, cos_r, sin_r), rot(x_col, cos_c, sin_c)], axis=-1).astype(x.dtype)

def sink_attend(scores, values, sink):
    B, KH, G, Q, _ = scores.shape
    sink_col = jnp.broadcast_to(sink.astype(F32)[None, :, :, None, None], (B, KH, G, Q, 1))
    p = jax.nn.softmax(jnp.concatenate([scores, sink_col], axis=-1), axis=-1)[..., :-1]
    return jnp.einsum('bkgqs,bskd->bqkgd', p.astype(values.dtype), values)

def window_gqa_mixer(h_lat, h_ctx, w_qkv, w_o, sinks, rope, need_ctx_out):
    B, S, _ = h_lat.shape
    q_dim = ATTN_HEADS * ATTN_HEAD_DIM
    kv_dim = ATTN_KV_HEADS * ATTN_HEAD_DIM
    scale = ATTN_HEAD_DIM ** -0.5
    sinks_g = sinks.reshape(ATTN_KV_HEADS, ATTN_GROUP)

    def project(h):
        b, t, _ = h.shape
        z = h @ w_qkv
        q = z[..., :q_dim].reshape(b, t, ATTN_KV_HEADS, ATTN_GROUP, ATTN_HEAD_DIM)
        k = z[..., q_dim:q_dim + kv_dim].reshape(b, t, ATTN_KV_HEADS, ATTN_HEAD_DIM)
        v = z[..., q_dim + kv_dim:].reshape(b, t, ATTN_KV_HEADS, ATTN_HEAD_DIM)
        return q, k, v

    q_l, k_l, v_l = project(h_lat)
    q_l, k_l = rope_2d(q_l, rope), rope_2d(k_l, rope)
    q_c, k_c, v_c = project(h_ctx)

    pad = ((0, 0), (ATTN_HALO, ATTN_HALO), (0, 0), (0, 0))
    k_pad, v_pad = jnp.pad(k_l, pad), jnp.pad(v_l, pad)
    span = ATTN_BLOCK + 2 * ATTN_HALO
    q_off = jnp.arange(ATTN_BLOCK)
    k_off = jnp.arange(span) - ATTN_HALO

    def block(start):
        qb = lax.dynamic_slice_in_dim(q_l, start, ATTN_BLOCK, axis=1)
        kb = lax.dynamic_slice_in_dim(k_pad, start, span, axis=1)
        vb = lax.dynamic_slice_in_dim(v_pad, start, span, axis=1)
        qpos, kpos = start + q_off, start + k_off
        valid = (jnp.abs(qpos[:, None] - kpos[None, :]) <= WINDOW) & (kpos[None, :] >= 0) & (kpos[None, :] < S)
        s_win = jnp.einsum('bqkgd,bskd->bkgqs', qb, kb).astype(F32) * scale
        s_win = jnp.where(valid, s_win, -jnp.inf)
        s_cx = jnp.einsum('bqkgd,bckd->bkgqc', qb, k_c).astype(F32) * scale
        return sink_attend(jnp.concatenate([s_win, s_cx], axis=-1),
                           jnp.concatenate([vb, v_c], axis=1), sinks_g)

    o = lax.map(block, jnp.arange(S // ATTN_BLOCK) * ATTN_BLOCK)
    y_lat = o.transpose(1, 0, 2, 3, 4, 5).reshape(B, S, q_dim) @ w_o
    y_ctx = None
    if need_ctx_out:
        s_cc = jnp.einsum('bqkgd,bckd->bkgqc', q_c, k_c).astype(F32) * scale
        o_c = sink_attend(s_cc, v_c, sinks_g)
        y_ctx = o_c.reshape(B, h_ctx.shape[1], q_dim) @ w_o
    return y_lat, y_ctx

def gla_chunked(q, k, v, log_a, s0):
    B, T, H, DK = q.shape
    DV = v.shape[-1]
    nc = T // GLA_CHUNK

    def chunks(a):
        return a.astype(F32).reshape(B, nc, GLA_CHUNK, H, a.shape[-1]).transpose(1, 0, 3, 2, 4)

    lower_tri = jnp.tril(jnp.ones((GLA_CHUNK, GLA_CHUNK), dtype=bool))[:, :, None]

    def step(state, inp):
        qi, ki, vi, gi = inp
        b = jnp.cumsum(gi, axis=2)
        b_end = b[:, :, -1:, :]
        o_inter = jnp.einsum('bhtk,bhkv->bhtv', qi * jnp.exp(b), state)
        diff = jnp.where(lower_tri, b[:, :, :, None, :] - b[:, :, None, :, :], -jnp.inf)
        scores = jnp.einsum('bhtk,bhsk,bhtsk->bhts', qi, ki, jnp.exp(diff))
        o_intra = jnp.einsum('bhts,bhsv->bhtv', scores, vi)
        new_state = state * jnp.exp(b_end[:, :, 0, :, None]) + jnp.einsum(
            'bhsk,bhsv->bhkv', ki * jnp.exp(b_end - b), vi)
        return new_state, o_inter + o_intra

    s_final, o = lax.scan(step, s0, (chunks(q), chunks(k), chunks(v), chunks(log_a)))
    o = o.transpose(1, 0, 3, 2, 4).reshape(B, T, H, DV).astype(v.dtype)
    return o, s_final

def gla_mixer(h_lat, h_ctx, w_in, w_a1, w_a2, b_a, norm_g, w_o, need_ctx_out):
    kd = GLA_HEADS * GLA_KEY_DIM
    vd = GLA_HEADS * GLA_VAL_DIM

    def project(h):
        b, t, _ = h.shape
        z = h @ w_in
        q = z[..., :kd].reshape(b, t, GLA_HEADS, GLA_KEY_DIM) * (GLA_KEY_DIM ** -0.5)
        k = z[..., kd:2 * kd].reshape(b, t, GLA_HEADS, GLA_KEY_DIM)
        v = z[..., 2 * kd:2 * kd + vd].reshape(b, t, GLA_HEADS, GLA_VAL_DIM)
        g = z[..., 2 * kd + vd:]
        log_a = [(jax.nn.log_sigmoid((h @ w_a1[d] @ w_a2[d] + b_a[d]).astype(F32)) / GLA_GATE_NORM)
                 .reshape(b, t, GLA_HEADS, GLA_KEY_DIM) for d in range(2)]
        return q, k, v, g, log_a

    def output(o, g):
        b, t = o.shape[:2]
        o = rmsnorm(o, norm_g).reshape(b, t, vd)
        return (o * jax.nn.silu(g)) @ w_o

    flip = lambda a: jnp.flip(a, axis=1)
    q_l, k_l, v_l, g_l, la_l = project(h_lat)
    q_c, k_c, v_c, g_c, la_c = project(h_ctx)
    B = h_lat.shape[0]
    s0 = jnp.zeros((B, GLA_HEADS, GLA_KEY_DIM, GLA_VAL_DIM), F32)
    o_cf, s_cf = gla_chunked(q_c, k_c, v_c, la_c[0], s0)
    o_lf, _ = gla_chunked(q_l, k_l, v_l, la_l[0], s_cf)
    o_cb, s_cb = gla_chunked(flip(q_c), flip(k_c), flip(v_c), flip(la_c[1]), s0)
    o_lb, _ = gla_chunked(flip(q_l), flip(k_l), flip(v_l), flip(la_l[1]), s_cb)
    y_lat = output(o_lf + flip(o_lb), g_l)
    y_ctx = output(o_cf + flip(o_cb), g_c) if need_ctx_out else None
    return y_lat, y_ctx

def grouped_moe(h, router_w, router_b, w_gate, w_up, w_down):
    N, D = h.shape
    scores = jax.nn.sigmoid(h.astype(F32) @ router_w.astype(F32))
    sel = (scores + router_b.astype(F32)).reshape(N, N_GROUPS, EXPERTS_PER_GROUP)
    group_score = lax.top_k(sel, TOP_K)[0].sum(-1)
    grp = jnp.argmax(group_score, axis=-1)
    sel_in = jnp.take_along_axis(sel, grp[:, None, None], axis=1)[:, 0]
    _, local = lax.top_k(sel_in, TOP_K)
    eidx = grp[:, None] * EXPERTS_PER_GROUP + local
    gate = jnp.take_along_axis(scores, eidx, axis=1)
    gate = gate / jnp.sum(gate, axis=-1, keepdims=True)
    A = N * TOP_K
    e_flat = eidx.reshape(A)
    order = jnp.argsort(e_flat)
    e_sorted = e_flat[order]
    tok_sorted = order // TOP_K
    gate_sorted = gate.reshape(A)[order].astype(h.dtype)
    counts = jnp.bincount(e_flat, length=N_EXPERTS)
    starts = jnp.cumsum(counts) - counts
    padded = (counts + MOE_BLOCK - 1) // MOE_BLOCK * MOE_BLOCK
    pends = jnp.cumsum(padded)
    pstarts = pends - padded
    slot = pstarts[e_sorted] + (jnp.arange(A) - starts[e_sorted])
    n_blocks = -(-A // MOE_BLOCK) + N_EXPERTS
    buf = jnp.zeros((n_blocks * MOE_BLOCK, D), h.dtype).at[slot].set(h[tok_sorted])
    block_expert = jnp.minimum(jnp.searchsorted(pends, jnp.arange(n_blocks) * MOE_BLOCK, side='right'),
                               N_EXPERTS - 1)

    def expert_block(args):
        xb, e = args
        hid = jax.nn.silu(xb @ w_gate[e]) * (xb @ w_up[e])
        return hid @ w_down[e]

    y_buf = lax.map(expert_block, (buf.reshape(n_blocks, MOE_BLOCK, D), block_expert)).reshape(-1, D)
    y = y_buf[slot] * gate_sorted[:, None]
    return jnp.zeros((N, D), h.dtype).at[tok_sorted].add(y)

def setup_inputs(seed: int = 0) -> dict:
    key = jax.random.key(seed)
    ks = jax.random.split(key, 23)

    def nrm(k, shape, scale):
        return jax.random.normal(k, shape, F32) * scale

    D = D_MODEL
    qkv_w = ATTN_HEADS * ATTN_HEAD_DIM + 2 * ATTN_KV_HEADS * ATTN_HEAD_DIM
    kd = GLA_HEADS * GLA_KEY_DIM
    vd = GLA_HEADS * GLA_VAL_DIM
    return {
        'x': nrm(ks[0], (BATCH, SEQ, D), 1.0),
        'c': nrm(ks[1], (BATCH, D), 1.0),
        'ctx': nrm(ks[2], (BATCH, CTX_LEN, D), 1.0),
        'c_ctx': nrm(ks[3], (D,), 1.0),
        'ada_w': nrm(ks[4], (DEPTH, D, 6 * D), 0.5 * D ** -0.5),
        'ada_b': nrm(ks[5], (DEPTH, 6 * D), 0.02),
        'norm_mix_g': 1.0 + nrm(ks[6], (DEPTH, D), 0.05),
        'norm_ffn_g': 1.0 + nrm(ks[7], (DEPTH, D), 0.05),
        'final_g': 1.0 + nrm(ks[8], (D,), 0.05),
        'attn_w_qkv': nrm(ks[9], (N_ATTN_LAYERS, D, qkv_w), D ** -0.5),
        'attn_w_o': nrm(ks[10], (N_ATTN_LAYERS, ATTN_HEADS * ATTN_HEAD_DIM, D), (ATTN_HEADS * ATTN_HEAD_DIM) ** -0.5),
        'attn_sinks': nrm(ks[11], (N_ATTN_LAYERS, ATTN_HEADS), 0.5),
        'gla_w_in': nrm(ks[12], (N_GLA_LAYERS, D, 2 * kd + 2 * vd), D ** -0.5),
        'gla_w_a1': nrm(ks[13], (N_GLA_LAYERS, 2, D, GLA_GATE_RANK), D ** -0.5),
        'gla_w_a2': nrm(ks[14], (N_GLA_LAYERS, 2, GLA_GATE_RANK, kd), GLA_GATE_RANK ** -0.5),
        'gla_b_a': nrm(ks[15], (N_GLA_LAYERS, 2, kd), 0.1),
        'gla_norm_g': 1.0 + nrm(ks[16], (N_GLA_LAYERS, GLA_VAL_DIM), 0.05),
        'gla_w_o': nrm(ks[17], (N_GLA_LAYERS, vd, D), vd ** -0.5),
        'router_w': nrm(ks[18], (D, N_EXPERTS), D ** -0.5),
        'router_b': nrm(ks[19], (N_EXPERTS,), 0.01),
        'moe_w_gate': nrm(ks[20], (DEPTH, N_EXPERTS, D, D_EXPERT), D ** -0.5),
        'moe_w_up': nrm(ks[21], (DEPTH, N_EXPERTS, D, D_EXPERT), D ** -0.5),
        'moe_w_down': nrm(ks[22], (DEPTH, N_EXPERTS, D_EXPERT, D), D_EXPERT ** -0.5),
    }

def reference(x, c, ctx, c_ctx, ada_w, ada_b, norm_mix_g, norm_ffn_g, final_g, attn_w_qkv, attn_w_o, attn_sinks,
              gla_w_in, gla_w_a1, gla_w_a2, gla_b_a, gla_norm_g, gla_w_o, router_w, router_b,
              moe_w_gate, moe_w_up, moe_w_down):
    B, S, D = x.shape
    C = ctx.shape[1]
    ROWS = S // GRID_W
    rope = axial_rope_tables(ROWS)
    silu_c = jax.nn.silu(c)
    silu_cc = jax.nn.silu(c_ctx)
    h_ctx_stream = ctx
    for i in range(DEPTH):
        last = i == DEPTH - 1
        mod_l = silu_c @ ada_w[i] + ada_b[i]
        mod_c = silu_cc @ ada_w[i] + ada_b[i]
        sh_m, sc_m, g_m, sh_f, sc_f, g_f = [m[:, None, :] for m in jnp.split(mod_l, 6, axis=-1)]
        csh_m, csc_m, cg_m, csh_f, csc_f, cg_f = jnp.split(mod_c, 6, axis=-1)
        h_l = modulate(rmsnorm(x, norm_mix_g[i]), sh_m, sc_m)
        h_c = modulate(rmsnorm(h_ctx_stream, norm_mix_g[i]), csh_m, csc_m)
        j = i // N_MIXERS
        if i % N_MIXERS == 0:
            y_l, y_c = window_gqa_mixer(h_l, h_c, attn_w_qkv[j], attn_w_o[j], attn_sinks[j], rope, not last)
        else:
            y_l, y_c = gla_mixer(h_l, h_c, gla_w_in[j], gla_w_a1[j], gla_w_a2[j], gla_b_a[j],
                                 gla_norm_g[j], gla_w_o[j], not last)
        x = x + g_m * y_l
        f_l = modulate(rmsnorm(x, norm_ffn_g[i]), sh_f, sc_f).reshape(B * S, D)
        if last:
            x = x + g_f * grouped_moe(f_l, router_w, router_b, moe_w_gate[i], moe_w_up[i],
                                      moe_w_down[i]).reshape(B, S, D)
        else:
            h_ctx_stream = h_ctx_stream + cg_m * y_c
            f_c = modulate(rmsnorm(h_ctx_stream, norm_ffn_g[i]), csh_f, csc_f).reshape(B * C, D)
            y_f = grouped_moe(jnp.concatenate([f_l, f_c], axis=0), router_w, router_b,
                              moe_w_gate[i], moe_w_up[i], moe_w_down[i])
            x = x + g_f * y_f[:B * S].reshape(B, S, D)
            h_ctx_stream = h_ctx_stream + cg_f * y_f[B * S:].reshape(B, C, D)
    return rmsnorm(x, final_g)


_drawn_inputs = setup_inputs


def setup_inputs(seed=0):
    import zlib

    import numpy as np

    out = dict(_drawn_inputs(seed))
    spreads = {}
    factors = {'attn_sinks': 8.0, 'gla_b_a': 3.99, 'gla_norm_g': 3.096}
    for name, (base, spread) in spreads.items():
        noise = np.random.default_rng([zlib.crc32(name.encode()), seed]).standard_normal(out[name].shape)
        drawn = base * np.exp(spread * noise) if base else spread * noise
        out[name] = __import__('jax').numpy.asarray(drawn.astype(out[name].dtype))
    for name, factor in factors.items():
        out[name] = (out[name] * factor).astype(out[name].dtype)
    return out
```

```python
from contextlib import ExitStack

import numpy as np
import concourse.bass as bass
from concourse import mybir
from concourse.alu_op_type import AluOpType as ALU

ACT = mybir.ActivationFunctionType
F32 = mybir.dt.float32
I32 = mybir.dt.int32
U32 = mybir.dt.uint32
AX = mybir.AxisListType.X

P = 128
D = 1024
KC = D // P
SEQ, CTX = 512, 256
NL, NX = SEQ // P, CTX // P
NT = NL + NX
GRID_W = 64
EPS = 1e-6
NEG = -1e30
PW = 512
RING = 3
HEADS, HD = 16, 64
GH, GK, GV = 4, 128, 256
RANK = 16
SUB = 32
NE, NG, EPG = 16, 4, 4
DE = 512
FC = DE // P
MAX_EXTRA = 12
NBLK = NE + MAX_EXTRA + 1


def constants():
    i, j = np.arange(P)[:, None], np.arange(P)[None, :]
    f = np.float32
    inv = (10000.0 ** (-np.arange(16, dtype=f) / f(16))).astype(f)
    pos = np.arange(SEQ)
    ang = np.stack([(pos // GRID_W).astype(f)[:, None] * inv, (pos % GRID_W).astype(f)[:, None] * inv], 1)
    c, s = np.cos(ang), np.sin(ang)
    cos = np.stack([c, c], 2).reshape(NL, P, HD).transpose(1, 0, 2).reshape(P, -1)
    sin = np.stack([-s, s], 2).reshape(NL, P, HD).transpose(1, 0, 2).reshape(P, -1)
    row = lambda v: np.tile(np.asarray(v, f)[None, :], (P, 1))
    parts = {
        "ident": (i == j), "ones": np.ones((P, P)), "before": (i < j),
        "mask_f": (i <= j), "mask_b": (i >= j),
        "cum_f": (i <= j) / 16.0, "cum_b": (i >= j) / 16.0,
        "tail_f": (i > j) / 16.0, "tail_b": (i < j) / 16.0, "sixteenth": np.full((P, 1), 1 / 16.0),
        "win": np.concatenate([np.where(j >= i, 0, NEG), np.where(j <= i, 0, NEG)], 1),
        "cos": cos, "sin": sin, "neghalf": np.full((P, 1), -0.5), "one": np.ones((P, 1)),
        "wins": row([3, 2, 1, 0] * 4), "e128": row(np.arange(NE) * 128), "idx": row(np.arange(16)),
    }
    off, out, n = {}, [], 0
    for k, v in parts.items():
        v = np.asarray(v, f)
        off[k] = (n, n + v.shape[1])
        n += v.shape[1]
        out.append(v)
    return np.ascontiguousarray(np.concatenate(out, 1)), off


class Region:

    def __init__(self, arena, at, end):
        self.arena, self.at, self.end = arena, at, end

    def take(self, *shape):
        n = int(np.prod(shape))
        ap = self.arena[:, self.at:self.at + n]
        self.at += n
        assert self.at <= self.end, (self.at, self.end)
        if len(shape) == 2:
            ap = ap.rearrange("p (a b) -> p a b", a=shape[0])
        elif len(shape) == 3:
            ap = ap.rearrange("p (a b c) -> p a b c", a=shape[0], b=shape[1])
        return ap


class Steps:

    def __init__(self, eng, sem):
        self.eng, self.sem, self.n, self.base = eng, sem, 0, None

    def __call__(self, ins):
        ins.then_inc(self.sem, 1)
        self.n += 1
        self.eng.wait_ge(self.sem, self.n if self.base is None else self.base + self.n)


def build(nc, a, out):
    with ExitStack() as ctx:
        sem = lambda name: ctx.enter_context(nc.semaphore(name))
        const_np, coff = constants()
        ncon = const_np.shape[1]
        ARENA = 52600
        arena = ctx.enter_context(nc.sbuf_tensor("arena", [P, ARENA], F32))
        slot_idx = ctx.enter_context(nc.sbuf_tensor("slot_idx", [P, NT * 2], U32))
        table_i = ctx.enter_context(nc.sbuf_tensor("table_i", [P, 32], I32))
        ps = [ctx.enter_context(nc.psum_tensor(f"bank{b}", [P, 512], F32)) for b in range(8)]

        mods = nc.dram_tensor("mods", [2, 2 * 6 * D], F32, kind="Internal").ap()
        xbuf = nc.dram_tensor("xbuf", [NBLK * P, D], F32, kind="Internal").ap()
        ybuf = nc.dram_tensor("ybuf", [NBLK * P, D], F32, kind="Internal").ap()

        fixed = Region(arena, 0, ARENA)
        ring = fixed.take(RING, KC * PW)
        X = fixed.take(NT, D)
        rows0 = fixed.at
        rows = fixed.take(6, D)
        hT0 = fixed.at
        hT = fixed.take(KC, NT * P)
        con = fixed.take(ncon)
        cT = fixed.take(KC, 2)
        csil = fixed.take(KC, 2)
        stat = fixed.take(256)
        R0 = fixed.at
        C = lambda k: con[:, coff[k][0]:coff[k][1]]
        ident, ones = C("ident"), C("ones")
        region = lambda at=R0, end=ARENA: Region(arena, at, end)
        ss, ms, rstd = stat[:, 0:32], stat[:, 32:64], stat[:, 64:96]

        r = region()
        mod_sb = r.take(2 * 6 * D)
        r = region()
        hbuf = r.take(2, D)
        junk = r.take(D)
        zb, rope_a, rope_b = r.take(2, 512), r.take(512), r.take(512)
        qT = r.take(KC, NT * P)
        kT = r.take(2, NT * P)
        V = r.take(NT, 256)
        prob, probT = r.take(2, 640), r.take(2, 640)
        att = r.take(2, 64)
        sinkrow = r.take(32)
        o_tok = region(hT0, R0).take(NT, D)
        oT = qT
        wo_tmp = r.take(512)
        r = region()
        H = r.take(NT, D)
        xg = r.take(D)
        xT = r.take(KC, P)
        sil, hid, hidT, ysb = r.take(DE), r.take(DE), r.take(FC, P), r.take(D)
        comb = r.take(4, D)
        rw = r.take(KC, NE)
        rt = Region(arena, r.at, r.at + 96 * 10 + 200)
        sc, sel, posn, s1, s2, M, t96, t96b, slot = [rt.take(NT, NE) for _ in range(9)]
        gs, gpos, g1, gt = [rt.take(NT, NG) for _ in range(4)]
        c1, c2, slotf = rt.take(NT), rt.take(NT), rt.take(NT, 2)
        r.at = rt.at
        cnt, ext, incl, t16, ovb, tab = [r.take(NE) for _ in range(5)] + [r.take(32)]
        big = r.take(MAX_EXTRA, NE)
        rbrow = r.take(NE)
        junk2 = comb[:, 0]
        r = region()
        hb_at = r.at
        r.take(2, D)
        zq = region(hb_at).take(2, 512)
        a2b = region(hb_at + 1024).take(2, 512)
        ktok, kTg, qTg, Vg, G = r.take(NT, 512), r.take(GH, SEQ), r.take(GH, SEQ), r.take(NT, D), r.take(NL, D)
        xc_at = RING * KC * PW + NL * D
        xc = region(xc_at, xc_at + NX * D)
        aT, wa1, gnrow = xc.take(2, NT * P), xc.take(KC, 2 * RANK), xc.take(GV)
        la = region(rows0, hT0).take(NT, 2, 512)
        r2 = region(hT0, hT0 + 6144)
        kp = [r2.take(4, 4, P) for _ in range(2)]
        bT, qh0 = r2.take(SEQ), r2.take(SEQ)
        scT0, scT1 = r2.take(NL, P), r2.take(NL, P)
        r3 = region(hb_at, hb_at + 2048)
        qh1, qp = r3.take(SEQ), r3.take(SEQ)
        khat = r3.take(NT, P)
        S_tmp = r3.take(GV)
        r4 = Region(arena, xc_at, xc_at + 2048)
        S = [r4.take(NL, GV) for _ in range(2)]
        qh, scT = [qh0, qh1], [scT0, scT1]
        r5 = region(hT0, R0)
        oTg, grow1, wo_tmp1 = r5.take(KC, SEQ), r5.take(D), r5.take(512)
        dec = stat[:, 96:104]
        ssg = stat[:, 104:112]
        msg = stat[:, 112:120]
        rsg = stat[:, 120:128]

        def panel(j):
            return ring[:, j % RING].rearrange("p (k n) -> p k n", k=KC)

        def down_panel(j):
            return ring[:, j % RING].rearrange("p (f n) -> p f n", f=FC)

        J_ADA, J_QKV = 0, 24
        J_WO0 = J_QKV + 3
        J_M0 = J_WO0 + 2
        J_GLA = J_M0 + 3
        J_WO1 = J_GLA + 6
        J_M1 = J_WO1 + 2

        consts_loaded, c_loaded, c_silu = sem("consts_loaded"), sem("c_loaded"), sem("c_silu")
        x_in, zeroed, zero_ready = sem("x_in"), sem("zeroed"), sem("zero_ready")
        panel_loaded = [sem(f"panel_loaded{s}") for s in range(RING)]
        mods_product, mods_added, mods_stored, bias_loaded = sem("mods_product"), sem("mods_added"), sem("mods_stored"), sem("bias_loaded")
        rows_loaded, rows_ready, small_loaded = sem("rows_loaded"), sem("rows_ready"), sem("small_loaded")
        phase_end = sem("phase_end")
        sumsq_ready, rstd_ready, normed, h_turned, hT_copied = sem("sumsq_ready"), sem("rstd_ready"), sem("normed"), sem("h_turned"), sem("hT_copied")
        act_steps, dve_steps, pool_steps = sem("act_steps"), sem("dve_steps"), sem("pool_steps")
        qkv_product, z_ready, qkv_turned, qkvT_copied = sem("qkv_product"), sem("z_ready"), sem("qkv_turned"), sem("qkvT_copied")
        scores_done, shift_ready, probs_ready = sem("scores_done"), sem("shift_ready"), sem("probs_ready")
        pa_turned, pb_turned, pa_copied, pb_copied = sem("pa_turned"), sem("pb_turned"), sem("pa_copied"), sem("pb_copied")
        pv_done, sinkarg_ready, sinkexp_ready, o_ready = sem("pv_done"), sem("sinkarg_ready"), sem("sinkexp_ready"), sem("o_ready")
        wo_product, wo_added = [sem("wo_product0"), sem("wo_product1")], [sem("wo_added0"), sem("wo_added1")]
        logits_done, gates_exp, picks_ready, ranks_done = sem("logits_done"), sem("gates_exp"), sem("picks_ready"), sem("ranks_done")
        table_ready, scattered = sem("table_ready"), sem("scattered")
        L = [{n: sem(f"{n}{l}") for n in (
            "x_loaded", "x_turned", "xT_act", "xT_dve", "gate_done", "up_done", "sil_ready", "hid_ready",
            "hid_turned", "hidT_ready", "down_done", "y0_ready", "y1_ready", "y_stored")} for l in range(2)]
        gathered = [sem("gathered_a"), sem("gathered_b")]
        combined = sem("combined")
        a_product, a_copied, z_product, ln_ready, la_ready = sem("a_product"), sem("a_copied"), sem("z_product"), sem("ln_ready"), sem("la_ready")
        gla_product, gla_evac, gla_turned, glaT_copied, silu_g = sem("gla_product"), sem("gla_evac"), sem("gla_turned"), sem("glaT_copied"), sem("silu_g")
        b_done, b_copied, tails_done, tails_exp = sem("b_done"), sem("b_copied"), sem("tails_done"), sem("tails_exp")
        args_ready, exps_ready, kq_ready, khat_ready = sem("args_ready"), sem("exps_ready"), sem("kq_ready"), sem("khat_ready")
        s_done, s_masked, p_done, state_ready, og_done = sem("s_done"), sem("s_masked"), sem("p_done"), sem("state_ready"), sem("og_done")
        og_sq, og_rstd, og_ready = sem("og_sq"), sem("og_rstd"), sem("og_ready")
        out_stored, ones_row = sem("out_stored"), sem("ones_row")
        SMALL = {"sinks": 16, "router": (48, 144), "gla": 96, "grow1": 112}

        NORM = {"mix0": (list(range(NT)), 0), "ffn0": (list(range(NT)), 6), "mix1": (list(range(NT)), 12),
                "ffn1": (list(range(NL)), 18), "final": (list(range(NL)), 22)}
        TURN = {"mix0": 0, "wo0": 6, "ffn0": 12, "mix1": 18, "wo1": 24, "ffn1": 28}
        MODULE = {"mix0": (0, 0, "norm_mix_g"), "ffn0": (0, 3, "norm_ffn_g"), "mix1": (1, 0, "norm_mix_g"), "ffn1": (1, 3, "norm_ffn_g")}
        ROWSEQ = ["mix0", "ffn0", "mix1", "ffn1", "final"]
        gla_steps = ([(0, t) for t in range(NL)] + [(1, t) for t in range(NT)] + [(n, t) for n in (2, 3) for t in range(NT)]
                     + [(n, t) for n in (4, 5) for t in range(NL)])
        gla_last = [max(m for m, (n, _) in enumerate(gla_steps) if n == k) + 1 for k in range(6)]
        turn_of = {m: i for i, m in enumerate([m for m, (n, t) in enumerate(gla_steps) if n < 2 and t < NL])}

        phases = {}

        def barrier(eng):
            phases[eng.engine] = phases.get(eng.engine, 0) + 1
            eng.drain().then_inc(phase_end, 1)
            eng.wait_ge(phase_end, 4 * phases[eng.engine])

        def wait_panel(eng, j, extra=None):
            n = 16 * (j // RING + 1)
            eng.wait_ge(panel_loaded[j % RING], n if extra is None else extra + n)

        block = ctx.enter_context(nc.Block())

        @block.sync
        def _(sp):
            sp.dma_start(con, a["const"]).then_inc(consts_loaded, 16)
            sp.dma_start(cT, a["cT"]).then_inc(c_loaded, 16)

            def load(j, src, k=KC):
                dst = panel(j) if k == KC else down_panel(j)
                sp.dma_start(dst, src).then_inc(panel_loaded[j % RING], 16)

            def cols(w, n):
                return w[:, n * PW:(n + 1) * PW].rearrange("(k p) n -> p k n", p=P)

            for j in range(24):
                if j >= RING:
                    sp.wait_ge(mods_product, j - RING + 1)
                load(j, cols(a["ada_w"][j // 12], j % 12))
            for n in range(3):
                sp.wait_ge(mods_product, J_QKV + n - RING + 1)
                load(J_QKV + n, cols(a["attn_w_qkv"][0], n))
            for n in range(2):
                sp.wait_ge(qkv_product, NT * (n + 1))
                load(J_WO0 + n, cols(a["attn_w_o"][0], n))

            def experts(l, j0, first_waits, extra):
                s = L[l]
                wg = a["moe_w_gate"][l].rearrange("e (k p) n -> e p k n", p=P)
                wu = a["moe_w_up"][l].rearrange("e (k p) n -> e p k n", p=P)
                wd = a["moe_w_down"][l].rearrange("e (f p) n -> e p f n", p=P)
                for n, w in enumerate((wg, wu, wd)):
                    first_waits[n]()
                    load(j0 + n, w[0], FC if n == 2 else KC)
                sp.wait_ge(table_ready, l + 1)
                nblk = sp.value_load(table_i[0:1, 31:32], min_val=NE, max_val=NE + MAX_EXTRA)
                sp.wait_ge(scattered, 16 * 2 * (NT if l == 0 else NT + NL))
                sp.dma_start(xg, xbuf[0:P, :]).then_inc(s["x_loaded"], 16)
                with sp.Fori(1, nblk) as i:
                    e = sp.value_load(table_i[0:1, bass.ds(i, 1)], min_val=0, max_val=NE - 1)
                    sp.wait_ge(s["x_turned"], i)
                    sp.dma_start(xg, xbuf[bass.ds(i * P, P), :]).then_inc(s["x_loaded"], 16)
                    for n, (w, used) in enumerate(((wg, "gate_done"), (wu, "up_done"), (wd, "down_done"))):
                        sp.wait_ge(s[used], i)
                        src = w[bass.ds(e, 1)].rearrange("o p k n -> (o p) k n")
                        load(j0 + n, src, FC if n == 2 else KC)
                sp.wait_ge(s["x_turned"], nblk)
                sp.dma_start(xg, xbuf[bass.ds(nblk * P, P), :]).then_inc(s["x_loaded"], 16)
                return nblk

            n0 = experts(0, J_M0, [lambda: sp.wait_ge(qkv_product, 3 * NT), lambda: sp.wait_ge(wo_product[0], NT),
                                   lambda: sp.wait_ge(wo_product[0], 2 * NT)], None)
            for n in range(6):
                if n < 3:
                    sp.wait_ge(L[0][("gate_done", "up_done", "down_done")[n]], n0)
                else:
                    sp.wait_ge(gla_product, gla_last[n - 3])
                load(J_GLA + n, cols(a["gla_w_in"][0], n))
            for n in range(2):
                sp.wait_ge(gla_product, gla_last[3 + n])
                load(J_WO1 + n, cols(a["gla_w_o"][0], n))
            experts(1, J_M1, [lambda: sp.wait_ge(gla_product, gla_last[5]), lambda: sp.wait_ge(wo_product[1], NL),
                              lambda: sp.wait_ge(wo_product[1], 2 * NL)], n0)
            for t in range(NL):
                sp.wait_ge(normed, NORM["final"][1] + t + 1)
                sp.dma_start(out[t * P:(t + 1) * P, :], H[:, t]).then_inc(out_stored, 16)
            sp.wait_ge(out_stored, 16 * NL)

        @block.gpsimd
        def _(pool):
            step = Steps(pool, pool_steps)
            step(nc.gpsimd.memset(arena[:, hT0:hT0 + D], 0.0))
            pool.wait_ge(consts_loaded, 16)
            for t in range(NT):
                src = a["x"][0, t * P:(t + 1) * P, :] if t < NL else a["ctx"][0, (t - NL) * P:(t - NL + 1) * P, :]
                pool.dma_start(X[:, t], src).then_inc(x_in, 16)
            pool.dma_start(mod_sb[0:2, :], a["ada_b"].rearrange("l n -> (l n)").unsqueeze(0).to_broadcast([2, 12 * D])).then_inc(bias_loaded, 16)
            for buf in (xbuf, ybuf):
                pool.dma_start(buf.rearrange("(b p) n -> p b n", p=P),
                               arena[:, hT0:hT0 + D].unsqueeze(1).to_broadcast([P, NBLK, D])).then_inc(zeroed, 16)
            pool.wait_ge(mods_added, 24)
            pool.dma_start(mods, mod_sb[0:2, :]).then_inc(mods_stored, 16)
            pool.wait_ge(mods_stored, 16)
            pool.wait_ge(zeroed, 16 * 2)

            loads = [0]

            def row_loads(name, gates):
                l, part, gain = MODULE[name]
                for stream in range(2):
                    for n, q in enumerate((part + 1, part)):
                        src = mods[stream:stream + 1, (l * 6 + q) * D:(l * 6 + q + 1) * D]
                        pool.dma_start(rows[:, 2 * stream + n], src.to_broadcast([P, D])).then_inc(rows_loaded, 16)
                gr = a[gain][l:l + 1, :].to_broadcast([P, D])
                pool.dma_start(arena[:, hT0:hT0 + D], gr).then_inc(rows_loaded, 16)
                if gates:
                    for stream in range(2):
                        src = mods[stream:stream + 1, (l * 6 + part + 2) * D:(l * 6 + part + 3) * D]
                        pool.dma_start(rows[:, 4 + stream], src.to_broadcast([P, D])).then_inc(rows_loaded, 16)

            def rstds(name):
                tiles, q0 = NORM[name]
                for q in range(q0, q0 + len(tiles)):
                    pool.wait_ge(sumsq_ready, q + 1)
                    step(nc.gpsimd.tensor_scalar(ms[:, q:q + 1], ss[:, q:q + 1], 1.0 / D, EPS, ALU.mult, ALU.add))
                    nc.gpsimd.tensor_tensor(rstd[:, q:q + 1], ms[:, q:q + 1], C("neghalf"), ALU.pow).then_inc(rstd_ready, 1)

            def small(dst, src):
                pool.dma_start(dst, src).then_inc(small_loaded, 16)

            def experts(l):
                T = NT if l == 0 else NL
                small(rw, a["router_w"].rearrange("(k p) e -> p k e", p=P))
                small(rbrow, a["router_b"].unsqueeze(0).to_broadcast([P, NE]))
                rstds(f"ffn{l}")
                pool.wait_ge(table_ready, l + 1)
                for t in range(T):
                    for c in range(2):
                        pool.indirect_dma_start(
                            out=xbuf[:, :], out_offset=bass.IndirectOffsetOnAxis(ap=slot_idx[:, 2 * t + c:2 * t + c + 1], axis=0),
                            in_=H[:, t], in_offset=None).then_inc(scattered, 16)
                barrier(pool)
                nblk = pool.value_load(table_i[0:1, 31:32], min_val=NE, max_val=NE + MAX_EXTRA)
                pool.wait_ge(L[l]["y_stored"], nblk * 16)
                step(nc.gpsimd.tensor_tensor(stat[:, 130:131], C("one"), C("one"), ALU.mult))
                for t in range(T):
                    m = t + (0 if l == 0 else NT)
                    if t >= 2:
                        pool.wait_ge(combined, m - 1)
                    for c in range(2):
                        pool.indirect_dma_start(
                            out=comb[:, 2 * (t % 2) + c], out_offset=None, in_=ybuf[:, :],
                            in_offset=bass.IndirectOffsetOnAxis(ap=slot_idx[:, 2 * t + c:2 * t + c + 1], axis=0)
                        ).then_inc(gathered[t % 2], 16)
                barrier(pool)

            barrier(pool)
            row_loads("mix0", True)
            rstds("mix0")
            barrier(pool)
            small(sinkrow[:, 0:HEADS], a["attn_sinks"].to_broadcast([P, HEADS]))
            barrier(pool)
            barrier(pool)
            barrier(pool)
            row_loads("ffn0", True)
            experts(0)
            row_loads("mix1", False)
            rstds("mix1")
            barrier(pool)
            small(wa1, a["wa1"])
            small(a2b[0:RANK + 1], a["a2b"])
            small(gnrow, a["gla_norm_g"].to_broadcast([P, GV]))
            barrier(pool)
            step(nc.gpsimd.memset(kp[0], 0.0))
            step(nc.gpsimd.memset(kp[1], 0.0))
            barrier(pool)
            for n in range(GH * NL):
                pool.wait_ge(og_sq, n + 1)
                step(nc.gpsimd.tensor_scalar(msg[:, n % 8:n % 8 + 1], ssg[:, n % 8:n % 8 + 1], 1.0 / GV, EPS, ALU.mult, ALU.add))
                nc.gpsimd.tensor_tensor(rsg[:, n % 8:n % 8 + 1], msg[:, n % 8:n % 8 + 1], C("neghalf"), ALU.pow).then_inc(og_rstd, 1)
            barrier(pool)
            small(grow1, mods[0:1, (6 + 2) * D:(6 + 3) * D].to_broadcast([P, D]))
            barrier(pool)
            row_loads("ffn1", True)
            experts(1)
            pool.dma_start(rows[:, 0], a["final_g"].unsqueeze(0).to_broadcast([P, D])).then_inc(rows_loaded, 16)
            rstds("final")

        @block.tensor
        def _(pe):
            def turn_tiles(name, src, ready_sem, ready0, T):
                for t in range(T):
                    g = TURN[name] + t
                    if ready_sem is not None:
                        pe.wait_ge(ready_sem, ready0 + t + 1)
                    if t >= 2:
                        pe.wait_ge(hT_copied, g - 1)
                    for k in range(KC):
                        mm = nc.tensor.transpose(ps[2 * (t % 2) + k // 4][:, (k % 4) * P:(k % 4 + 1) * P],
                                                 src(t)[:, k * P:(k + 1) * P], ident)
                    mm.then_inc(h_turned, 1)

            def product(bank, lhsT, rhs, n=KC):
                for k in range(n):
                    mm = nc.tensor.matmul(bank, lhsT(k), rhs(k), start=(k == 0), stop=(k == n - 1))
                return mm

            def out_project(l, oTx, T, j0, extra):
                for n in range(2):
                    wait_panel(pe, j0 + n, extra)
                    for t in range(T):
                        m = n * T + t
                        if m >= 4:
                            pe.wait_ge(wo_added[l], m - 3)
                        product(ps[4 + m % 4][:], lambda k: oTx[:, k, t * P:(t + 1) * P],
                                lambda k: panel(j0 + n)[:, k, :]).then_inc(wo_product[l], 1)

            def experts(l, j0, extra):
                T = NT if l == 0 else NL
                s = L[l]
                pe.wait_ge(small_loaded, SMALL["router"][l])
                pe.wait_ge(hT_copied, TURN[f"ffn{l}"] + T)
                for t in range(T):
                    mm = product(ps[4][:, t * NE:(t + 1) * NE], lambda k: hT[:, k, t * P:(t + 1) * P], lambda k: rw[:, k, :])
                mm.then_inc(logits_done, 1)
                pe.wait_ge(picks_ready, l + 1)
                for t in range(T):
                    for t2 in range(t):
                        nc.tensor.matmul(ps[5][:, t * NE:(t + 1) * NE], ones, M[:, t2], start=(t2 == 0), stop=False)
                    nc.tensor.matmul(ps[5][:, t * NE:(t + 1) * NE], C("before"), M[:, t], start=(t == 0), stop=True)
                mm = product(ps[6][:, 0:NE], lambda t: ones, lambda t: M[:, t], T)
                mm.then_inc(ranks_done, 1)
                barrier(pe)
                nblk = pe.value_load(table_i[0:1, 31:32], min_val=NE, max_val=NE + MAX_EXTRA)
                gp, up, dp = panel(j0), panel(j0 + 1), down_panel(j0 + 2)

                def turn_block():
                    for k in range(KC):
                        mm = nc.tensor.transpose(ps[k // 4][:, (k % 4) * P:(k % 4 + 1) * P], xg[:, k * P:(k + 1) * P], ident)
                    mm.then_inc(s["x_turned"], 1)

                pe.wait_ge(s["x_loaded"], 16)
                turn_block()
                with pe.Fori(0, nblk) as i:
                    i16 = i * 16 if extra is None else i * 16 + extra
                    pe.wait_ge(s["xT_act"], i + 1)
                    pe.wait_ge(s["xT_dve"], i + 1)
                    wait_panel(pe, j0, i16)
                    product(ps[2][:], lambda k: xT[:, k, :], lambda k: gp[:, k, :]).then_inc(s["gate_done"], 1)
                    wait_panel(pe, j0 + 1, i16)
                    product(ps[3][:], lambda k: xT[:, k, :], lambda k: up[:, k, :]).then_inc(s["up_done"], 1)
                    pe.wait_ge(s["x_loaded"], i * 16 + 32)
                    turn_block()
                    pe.wait_ge(s["hid_ready"], i + 1)
                    for f in range(FC):
                        mm = nc.tensor.transpose(ps[4][:, f * P:(f + 1) * P], hid[:, f * P:(f + 1) * P], ident)
                    mm.then_inc(s["hid_turned"], 1)
                    pe.wait_ge(s["hidT_ready"], i + 1)
                    wait_panel(pe, j0 + 2, i16)
                    product(ps[5][:], lambda f: hidT[:, f, :], lambda f: dp[:, f, 0:512], FC)
                    product(ps[6][:], lambda f: hidT[:, f, :], lambda f: dp[:, f, 512:1024], FC).then_inc(s["down_done"], 1)
                barrier(pe)
                return nblk

            pe.wait_ge(consts_loaded, 16)
            pe.wait_ge(c_silu, 2)
            for j in range(24):
                wait_panel(pe, j)
                if j >= 2:
                    pe.wait_ge(mods_added, j - 1)
                product(ps[j % 2][0:2, :], lambda k: csil[:, k, :], lambda k: panel(j)[:, k, :]).then_inc(mods_product, 1)
            barrier(pe)
            turn_tiles("mix0", lambda t: hbuf[:, t % 2], normed, NORM["mix0"][1], NT)
            barrier(pe)

            def turn_z(m):
                n = m // NT
                pe.wait_ge(z_ready, m + 1)
                if m >= 2:
                    pe.wait_ge(qkvT_copied, m - 1)
                for c in range(4 if n < 2 else 2):
                    mm = nc.tensor.transpose(ps[2 + m % 2][:, c * P:(c + 1) * P], zb[:, m % 2, c * P:(c + 1) * P], ident)
                mm.then_inc(qkv_turned, 1)

            for m in range(3 * NT + 1):
                if m < 3 * NT:
                    n, t = divmod(m, NT)
                    if t == 0:
                        wait_panel(pe, J_QKV + n)
                    if m >= 2:
                        pe.wait_ge(z_ready, m - 1)
                    product(ps[m % 2][:], lambda k: hT[:, k, t * P:(t + 1) * P], lambda k: panel(J_QKV + n)[:, k, :]).then_inc(qkv_product, 1)
                if m >= 1:
                    turn_z(m - 1)
            barrier(pe)

            U = NT * HEADS

            def scores(u):
                t, h = divmod(u, HEADS)
                n, par, c = h // 8, (h % 8) // 4, h % 4
                q = qT[64 * par:64 * par + 64, n * 4 + c, t * P:(t + 1) * P]
                kk = lambda c0, c1: kT[64 * par:64 * par + 64, n, c0:c1]
                if u >= 2:
                    pe.wait_ge(probs_ready, u - 1)
                if t < NL:
                    nc.tensor.matmul(ps[u % 2][:, 0:P], q, kk(t * P, (t + 1) * P), start=True, stop=True)
                    nc.tensor.matmul(ps[u % 2][:, P:P + CTX], q, kk(SEQ, SEQ + CTX), start=True, stop=True)
                    b = ps[2 + u % 2]
                    if 0 < t < NL - 1:
                        nc.tensor.matmul(b[:, 0:P], q, kk((t - 1) * P, t * P), start=True, stop=True)
                        mm = nc.tensor.matmul(b[:, P:2 * P], q, kk((t + 1) * P, (t + 2) * P), start=True, stop=True)
                    else:
                        o = t + 1 if t == 0 else t - 1
                        mm = nc.tensor.matmul(b[:, 0:P], q, kk(o * P, (o + 1) * P), start=True, stop=True)
                else:
                    mm = nc.tensor.matmul(ps[u % 2][:, 0:CTX], q, kk(SEQ, SEQ + CTX), start=True, stop=True)
                mm.then_inc(scores_done, 1)

            def turn_probs(u):
                t = u // HEADS
                pe.wait_ge(probs_ready, u + 1)
                if u >= 1:
                    pe.wait_ge(pa_copied, u)
                for c in range(3 if t < NL else 2):
                    mm = nc.tensor.transpose(ps[4][:, c * P:(c + 1) * P], prob[:, u % 2, c * P:(c + 1) * P], ident)
                mm.then_inc(pa_turned, 1)
                if t < NL:
                    if u >= 1:
                        pe.wait_ge(pb_copied, u)
                    for c in range(2 if 0 < t < NL - 1 else 1):
                        mm = nc.tensor.transpose(ps[5][:, c * P:(c + 1) * P], prob[:, u % 2, (3 + c) * P:(4 + c) * P], ident)
                    mm.then_inc(pb_turned, 1)

            def values(u):
                t, h = divmod(u, HEADS)
                hh = u // 8
                if t < NL:
                    keys = [t, NL, NL + 1] + ([t - 1, t + 1] if 0 < t < NL - 1 else [t + 1 if t == 0 else t - 1])
                    pe.wait_ge(pb_copied, u + 1)
                else:
                    keys = [NL, NL + 1]
                pe.wait_ge(pa_copied, u + 1)
                if h % 8 == 0 and hh >= 2:
                    pe.wait_ge(o_ready, hh - 1)
                g = h // 4
                product(ps[6 + hh % 2][:, (h % 8) * HD:(h % 8 + 1) * HD],
                        lambda b: probT[:, u % 2, b * P:(b + 1) * P],
                        lambda b: V[:, keys[b], g * HD:(g + 1) * HD], len(keys)).then_inc(pv_done, 1)

            for u in range(U + 2):
                if u < U:
                    scores(u)
                if 1 <= u <= U:
                    turn_probs(u - 1)
                if u >= 2:
                    values(u - 2)
            barrier(pe)
            turn_tiles("wo0", lambda t: o_tok[:, t], None, 0, NT)
            pe.wait_ge(hT_copied, TURN["wo0"] + NT)
            out_project(0, oT, NT, J_WO0, None)
            barrier(pe)
            turn_tiles("ffn0", lambda t: H[:, t], normed, NORM["ffn0"][1], NT)
            n0 = experts(0, J_M0, None)
            extra = n0 * 16 - 16
            turn_tiles("mix1", lambda t: hbuf[:, t % 2], normed, NORM["mix1"][1], NT)
            barrier(pe)

            pe.wait_ge(small_loaded, SMALL["gla"])
            for d in range(2):
                product(ps[2 * d][0:RANK, :], lambda k: wa1[:, k, d * RANK:(d + 1) * RANK], lambda k: hT[:, k, 0:SEQ])
                product(ps[2 * d + 1][0:RANK, 0:CTX], lambda k: wa1[:, k, d * RANK:(d + 1) * RANK],
                        lambda k: hT[:, k, SEQ:SEQ + CTX]).then_inc(a_product, 1)
            pe.wait_ge(a_copied, 4)
            for n in range(2 * NT):
                t, d = divmod(n, 2)
                if n >= 2:
                    pe.wait_ge(la_ready, n - 1)
                nc.tensor.matmul(ps[4 + n % 2][:], aT[0:RANK + 1, d, t * P:(t + 1) * P], a2b[0:RANK + 1, d, :],
                                 start=True, stop=True).then_inc(z_product, 1)

            def turn_gla(m):
                n, t = gla_steps[m]
                i = turn_of[m]
                pe.wait_ge(gla_evac, m + 1)
                if i >= 2:
                    pe.wait_ge(glaT_copied, i - 1)
                src = zq[:, m % 2] if n == 0 else ktok[:, t]
                for c in range(GH):
                    mm = nc.tensor.transpose(ps[2 + i % 2][:, c * P:(c + 1) * P], src[:, c * P:(c + 1) * P], ident)
                mm.then_inc(gla_turned, 1)

            NS = len(gla_steps)
            for m in range(NS):
                n, t = gla_steps[m]
                if t == 0:
                    wait_panel(pe, J_GLA + n, extra)
                if m >= 2:
                    pe.wait_ge(gla_evac, m - 1)
                product(ps[6 + m % 2][:], lambda k: hT[:, k, t * P:(t + 1) * P], lambda k: panel(J_GLA + n)[:, k, :]).then_inc(gla_product, 1)
                if m >= 1 and (m - 1) in turn_of:
                    turn_gla(m - 1)
            barrier(pe)
            barrier(pe)

            for u in range(2 * GH):
                h, d = divmod(u, 2)
                cum, tail = (C("cum_f"), C("tail_f")) if d == 0 else (C("cum_b"), C("tail_b"))
                lac = lambda t: la[:, t, d, h * GK:(h + 1) * GK]
                if u >= 1:
                    pe.wait_ge(b_copied, u)
                    pe.wait_ge(tails_exp, u)
                for t in range(NL):
                    mm = nc.tensor.matmul(ps[0][:, t * P:(t + 1) * P], lac(t), cum, start=True, stop=True)
                mm.then_inc(b_done, 1)
                for t in range(NT):
                    bank = ps[1][:, t * P:(t + 1) * P] if t < 4 else ps[2][:, (t - 4) * P:(t - 3) * P]
                    nc.tensor.matmul(bank, tail, lac(t), start=True, stop=True)
                for t in range(NT):
                    mm = nc.tensor.matmul(ps[2][:, 256 + t:257 + t], lac(t), C("sixteenth"), start=True, stop=True)
                mm.then_inc(tails_done, 1)
                order = [4, 5, 0, 1, 2] if d == 0 else [5, 4, 3, 2, 1]
                pe.wait_ge(khat_ready, u + 1)
                for n, t in enumerate(order):
                    k = 5 * u + n
                    if k >= 2:
                        pe.wait_ge(state_ready, k - 1)
                    nc.tensor.matmul(ps[4 + k % 2][:, 0:GV], khat[:, t, :], Vg[:, t, h * GV:(h + 1) * GV],
                                     start=True, stop=True).then_inc(p_done, 1)
                pe.wait_ge(kq_ready, u + 1)
                if u >= 1:
                    pe.wait_ge(s_masked, u)
                for t in range(NL):
                    for i in range(P // SUB):
                        mm = nc.tensor.matmul(ps[3][:, t * P + i * SUB:t * P + (i + 1) * SUB], kp[d][:, t, i, :],
                                              qp[:, t * P + i * SUB:t * P + (i + 1) * SUB], start=True, stop=True)
                mm.then_inc(s_done, 1)
                if d == 1:
                    pe.wait_ge(s_masked, u + 1)
                    pe.wait_ge(state_ready, 5 * (u + 1))
                    for t in range(NL):
                        k = h * NL + t
                        if k >= 2:
                            pe.wait_ge(og_ready, k - 1)
                        o = ps[6 + k % 2][:, 0:GV]
                        v = Vg[:, t, h * GV:(h + 1) * GV]
                        for dd in range(2):
                            nc.tensor.matmul(o, qh[dd][:, t * P:(t + 1) * P], S[dd][:, t, :], start=(dd == 0), stop=False)
                            mm = nc.tensor.matmul(o, scT[dd][:, t, :], v, start=False, stop=(dd == 1))
                        mm.then_inc(og_done, 1)
            barrier(pe)
            turn_tiles("wo1", lambda t: G[:, t], None, 0, NL)
            pe.wait_ge(hT_copied, TURN["wo1"] + NL)
            out_project(1, oTg, NL, J_WO1, extra)
            barrier(pe)
            turn_tiles("ffn1", lambda t: H[:, t], normed, NORM["ffn1"][1], NL)
            experts(1, J_M1, extra)

        @block.scalar
        def _(act):
            step = Steps(act, act_steps)
            act.wait_ge(c_loaded, 16)
            act.wait_ge(consts_loaded, 16)
            nc.scalar.activation(csil, cT, ACT.Exp, scale=-1.0).then_inc(c_silu, 1)

            def squares(name):
                tiles, q0 = NORM[name]
                jk = junk if name.startswith("mix") else junk2
                for t in tiles:
                    q = q0 + t
                    nc.scalar.activation(jk, X[:, t], ACT.Square, accum_out=ss[:, q:q + 1]).then_inc(sumsq_ready, 1)
                    act.wait_ge(sumsq_ready, q + 1)

            def copy_turned(name, dst, T):
                for t in range(T):
                    g = TURN[name] + t
                    act.wait_ge(h_turned, g + 1)
                    for half in range(2):
                        ins = nc.scalar.copy(dst[:, 4 * half:4 * half + 4, t * P:(t + 1) * P],
                                             ps[2 * (t % 2) + half][:].rearrange("p (k n) -> p k n", k=4))
                        if half:
                            ins.then_inc(hT_copied, 1)
                        else:
                            step(ins)

            def experts(l):
                s = L[l]
                squares(f"ffn{l}")
                copy_turned(f"ffn{l}", hT, NT if l == 0 else NL)
                T = NT if l == 0 else NL
                act.wait_ge(logits_done, l + 1)
                nc.scalar.activation(sc[:, 0:T].rearrange("p a b -> p (a b)"), ps[4][:, 0:T * NE], ACT.Exp, scale=-1.0).then_inc(gates_exp, 1)
                barrier(act)
                nblk = act.value_load(table_i[0:1, 31:32], min_val=NE, max_val=NE + MAX_EXTRA)

                def copy_xT():
                    return nc.scalar.copy(xT[:, 0:4, :], ps[0][:].rearrange("p (k n) -> p k n", k=4))

                act.wait_ge(s["x_turned"], 1)
                copy_xT().then_inc(s["xT_act"], 1)
                with act.Fori(0, nblk) as i:
                    act.wait_ge(s["gate_done"], i + 1)
                    nc.scalar.activation(sil, ps[2][:], ACT.Silu).then_inc(s["sil_ready"], 1)
                    act.wait_ge(s["x_turned"], i + 2)
                    copy_xT().then_inc(s["xT_act"], 1)
                    act.wait_ge(s["hid_turned"], i + 1)
                    nc.scalar.copy(hidT.rearrange("p f n -> p (f n)"), ps[4][:]).then_inc(s["hidT_ready"], 1)
                    act.wait_ge(s["down_done"], i + 1)
                    nc.scalar.copy(ysb[:, 0:512], ps[5][:]).then_inc(s["y0_ready"], 1)
                    act.wait_ge(s["y0_ready"], i + 1)
                    act.wait_ge(s["y1_ready"], i + 1)
                    act.dma_start(ybuf[bass.ds(i * P, P), :], ysb).then_inc(s["y_stored"], 16)
                    act.wait_ge(s["y_stored"], i * 16 + 16)
                barrier(act)

            barrier(act)
            act.wait_ge(x_in, 16 * NT)
            squares("mix0")
            copy_turned("mix0", hT, NT)
            barrier(act)
            for m in range(3 * NT):
                n, t = divmod(m, NT)
                act.wait_ge(qkv_turned, m + 1)
                if n < 2:
                    ins = nc.scalar.copy(qT[:, 4 * n:4 * n + 4, t * P:(t + 1) * P], ps[2 + m % 2][:].rearrange("p (k n) -> p k n", k=4))
                else:
                    ins = nc.scalar.copy(kT[:, :, t * P:(t + 1) * P], ps[2 + m % 2][:, 0:256].rearrange("p (k n) -> p k n", k=2))
                ins.then_inc(qkvT_copied, 1)
            barrier(act)

            U = NT * HEADS
            for u in range(U + 1):
                t, h = divmod(u, HEADS)
                if u < U:
                    st = att[:, (u // 8) % 2]
                    hi = h % 8
                    act.wait_ge(shift_ready, u + 1)
                    if u >= 2:
                        act.wait_ge(pa_turned, u - 1)
                    if hi == 0 and u >= 16:
                        act.wait_ge(o_ready, u // 8 - 1)
                    na = 384 if t < NL else 256
                    a1 = nc.scalar.activation(prob[:, u % 2, 0:na], ps[u % 2][:, 0:na], ACT.Exp, bias=st[:, 8 + hi:9 + hi],
                                              scale=HD ** -0.5, accum_out=st[:, 16 + hi:17 + hi])
                    if t < NL:
                        step(a1)
                        nb = 256 if 0 < t < NL - 1 else 128
                        a1 = nc.scalar.activation(prob[:, u % 2, 384:384 + nb], prob[:, u % 2, 384:384 + nb], ACT.Exp,
                                                  bias=st[:, 8 + hi:9 + hi], scale=HD ** -0.5, accum_out=st[:, 24 + hi:25 + hi])
                    a1.then_inc(probs_ready, 1)
                if u >= 1:
                    v = u - 1
                    tv = v // HEADS
                    act.wait_ge(pa_turned, v + 1)
                    if v >= 2:
                        act.wait_ge(pv_done, v - 1)
                    na = 384 if tv < NL else 256
                    nc.scalar.copy(probT[:, v % 2, 0:na], ps[4][:, 0:na]).then_inc(pa_copied, 1)
                    if v % 8 == 7:
                        hh = v // 8
                        sv = att[:, hh % 2]
                        act.wait_ge(sinkarg_ready, hh + 1)
                        nc.scalar.activation(sv[:, 32:40], sv[:, 32:40], ACT.Exp).then_inc(sinkexp_ready, 1)
            barrier(act)
            copy_turned("wo0", oT, NT)
            barrier(act)
            experts(0)
            squares("mix1")
            copy_turned("mix1", hT, NT)
            barrier(act)
            act.wait_ge(ones_row, 1)
            for d in range(2):
                act.wait_ge(a_product, d + 1)
                nc.scalar.copy(aT[0:RANK, d, 0:SEQ], ps[2 * d][0:RANK, :]).then_inc(a_copied, 1)
                nc.scalar.copy(aT[0:RANK, d, SEQ:SEQ + CTX], ps[2 * d + 1][0:RANK, 0:CTX]).then_inc(a_copied, 1)
            for n in range(2 * NT):
                t, d = divmod(n, 2)
                l1 = la[:, t, d, :]
                act.wait_ge(z_product, n + 1)
                step(nc.scalar.activation(l1, ps[4 + n % 2][:], ACT.Abs))
                step(nc.scalar.activation(l1, l1, ACT.Exp, scale=-1.0))
                nc.scalar.activation(l1, l1, ACT.Ln, bias=C("one")).then_inc(ln_ready, 1)
            for m in range(len(gla_steps)):
                n, t = gla_steps[m]
                if m in turn_of:
                    i = turn_of[m]
                    act.wait_ge(gla_turned, i + 1)
                    dst = (qTg if n == 0 else kTg)[:, :, t * P:(t + 1) * P]
                    nc.scalar.copy(dst, ps[2 + i % 2][:].rearrange("p (k n) -> p k n", k=4)).then_inc(glaT_copied, 1)
                if n >= 4:
                    act.wait_ge(gla_product, m + 1)
                    nc.scalar.activation(G[:, t, (n - 4) * 512:(n - 3) * 512], ps[6 + m % 2][:], ACT.Silu).then_inc(silu_g, 1)
            barrier(act)
            barrier(act)
            for u in range(2 * GH):
                h, d = divmod(u, 2)
                act.wait_ge(b_done, u + 1)
                if u >= 1:
                    act.wait_ge(kq_ready, u)
                nc.scalar.copy(bT, ps[0][:]).then_inc(b_copied, 1)
                act.wait_ge(tails_done, u + 1)
                if u >= 1:
                    act.wait_ge(p_done, 5 * u)
                    act.wait_ge(state_ready, 5 * u)
                step(nc.scalar.activation(khat[:, 0:4, :].rearrange("p a b -> p (a b)"), ps[1][:], ACT.Exp))
                step(nc.scalar.activation(khat[:, 4:6, :].rearrange("p a b -> p (a b)"), ps[2][:, 0:256], ACT.Exp))
                nc.scalar.activation(dec[:, 0:NT], ps[2][:, 256:256 + NT], ACT.Exp).then_inc(tails_exp, 1)
                if u >= 2:
                    act.wait_ge(og_done, NL * (h))
                act.wait_ge(b_copied, u + 1)
                step(nc.scalar.activation(qh[d], bT, ACT.Exp))
                act.wait_ge(args_ready, u + 1)
                step(nc.scalar.activation(qp, qp, ACT.Exp))
                for i in range(4):
                    k0, k1 = (0, SUB * (i + 1)) if d == 0 else (SUB * i, P)
                    ins = nc.scalar.activation(kp[d][:, :, i, k0:k1], kp[d][:, :, i, k0:k1], ACT.Exp)
                    if i < 3:
                        step(ins)
                ins.then_inc(exps_ready, 1)
                if d == 1:
                    for t in range(NL):
                        k = h * NL + t
                        act.wait_ge(og_done, k + 1)
                        if k >= 8:
                            act.wait_ge(og_ready, k - 7)
                        nc.scalar.activation(S[1][:, t, :], ps[6 + k % 2][:, 0:GV], ACT.Square, accum_out=ssg[:, k % 8:k % 8 + 1]).then_inc(og_sq, 1)
                        act.wait_ge(og_sq, k + 1)
            barrier(act)
            copy_turned("wo1", oTg, NL)
            barrier(act)
            experts(1)
            squares("final")

        @block.vector
        def _(dve):
            step = Steps(dve, dve_steps)
            dve.wait_ge(c_silu, 1)
            dve.wait_ge(consts_loaded, 16)
            step(nc.vector.tensor_scalar(csil, csil, 1.0, None, ALU.add))
            step(nc.vector.reciprocal(csil, csil))
            nc.vector.tensor_tensor(csil, csil, cT, ALU.mult).then_inc(c_silu, 1)
            dve.wait_ge(bias_loaded, 16)
            for j in range(24):
                dve.wait_ge(mods_product, j + 1)
                m = mod_sb[0:2, j * PW:(j + 1) * PW]
                nc.vector.tensor_tensor(m, ps[j % 2][0:2, :], m, ALU.add).then_inc(mods_added, 1)
            barrier(dve)
            rowcount = [0]

            def prepare_rows(name, gates):
                rowcount[0] += 5 + 2 * gates
                dve.wait_ge(rows_loaded, 16 * rowcount[0])
                for stream in range(2):
                    step(nc.vector.scalar_tensor_tensor(out=rows[:, 2 * stream], in0=rows[:, 2 * stream], scalar=1.0,
                                                        in1=arena[:, hT0:hT0 + D], op0=ALU.add, op1=ALU.mult))
                nc.vector.memset(stat[:, 128:129], 0.0).then_inc(rows_ready, 1)

            def norms(name):
                tiles, q0 = NORM[name]
                for t in tiles:
                    q = q0 + t
                    st = 0 if t < NL else 1
                    dve.wait_ge(rstd_ready, q + 1)
                    if name.startswith("mix"):
                        if t >= 2:
                            dve.wait_ge(h_turned, TURN[name] + t - 1)
                        h = hbuf[:, t % 2]
                    else:
                        h = H[:, t]
                    if name == "final":
                        nc.vector.scalar_tensor_tensor(out=h, in0=X[:, t], scalar=rstd[:, q:q + 1], in1=rows[:, 0],
                                                       op0=ALU.mult, op1=ALU.mult).then_inc(normed, 1)
                        continue
                    step(nc.vector.scalar_tensor_tensor(out=h, in0=X[:, t], scalar=rstd[:, q:q + 1], in1=rows[:, 2 * st],
                                                        op0=ALU.mult, op1=ALU.mult))
                    nc.vector.tensor_tensor(h, h, rows[:, 2 * st + 1], ALU.add).then_inc(normed, 1)

            def out_project(l, T, grow, tmp):
                for m in range(2 * T):
                    n, t = divmod(m, T)
                    dve.wait_ge(wo_product[l], m + 1)
                    step(nc.vector.tensor_tensor(tmp, ps[4 + m % 4][:], grow(t)[:, n * 512:(n + 1) * 512], ALU.mult))
                    xs = X[:, t, n * 512:(n + 1) * 512]
                    nc.vector.tensor_tensor(xs, xs, tmp, ALU.add).then_inc(wo_added[l], 1)
                    dve.wait_ge(wo_added[l], m + 1)

            def places(pos, s, g):
                for dl in (1, 2, 3):
                    step(nc.vector.tensor_tensor(g[:, :, 0:4 - dl], s[:, :, 0:4 - dl], s[:, :, dl:4], ALU.is_ge))
                    step(nc.vector.tensor_tensor(pos[:, :, dl:4], pos[:, :, dl:4], g[:, :, 0:4 - dl], ALU.add))
                    step(nc.vector.tensor_tensor(pos[:, :, 0:4 - dl], pos[:, :, 0:4 - dl], g[:, :, 0:4 - dl], ALU.subtract))

            def route(l):
                T = NT if l == 0 else NL
                tt, ts_ = nc.vector.tensor_tensor, nc.vector.tensor_scalar
                fl = lambda v: v[:, 0:T].rearrange("p a b -> p (a b)")
                gv = lambda v: fl(v).rearrange("p (g e) -> p g e", e=EPG)
                bc = lambda row: row.unsqueeze(1).to_broadcast([P, T, row.shape[1]])
                dve.wait_ge(gates_exp, l + 1)
                dve.wait_ge(small_loaded, SMALL["router"][l])
                step(ts_(fl(sc), fl(sc), 1.0, None, ALU.add))
                step(nc.vector.reciprocal(fl(sc), fl(sc)))
                step(tt(sel[:, 0:T], sc[:, 0:T], bc(rbrow), ALU.add))
                step(nc.vector.tensor_copy(posn[:, 0:T], bc(C("wins"))))
                places(gv(posn), gv(sel), gv(t96))
                step(ts_(fl(t96), fl(posn), 1.5, None, ALU.is_lt))
                step(tt(fl(t96b), fl(t96), fl(sel), ALU.mult))
                gflat = lambda v: v[:, 0:T].rearrange("p a b -> p (a b)")
                step(nc.vector.tensor_reduce(gflat(gs), gv(t96b), AX, ALU.add))
                step(nc.vector.tensor_copy(gpos[:, 0:T], bc(C("wins")[:, 0:NG])))
                places(gpos[:, 0:T], gs[:, 0:T], gt[:, 0:T])
                step(ts_(gflat(g1), gflat(gpos), 0.5, None, ALU.is_lt))
                g1b = gflat(g1).unsqueeze(2).to_broadcast([P, T * NG, EPG])
                step(ts_(fl(s1), fl(posn), 0.5, None, ALU.is_lt))
                step(tt(fl(s2), fl(t96), fl(s1), ALU.subtract))
                step(tt(gv(s1), gv(s1), g1b, ALU.mult))
                step(tt(gv(s2), gv(s2), g1b, ALU.mult))
                tt(fl(M), fl(s1), fl(s2), ALU.add).then_inc(picks_ready, 1)
                step(tt(fl(t96), fl(sc), fl(s1), ALU.mult))
                step(nc.vector.tensor_reduce(c1[:, 0:T], t96[:, 0:T], AX, ALU.add))
                step(tt(fl(t96), fl(sc), fl(s2), ALU.mult))
                step(nc.vector.tensor_reduce(c2[:, 0:T], t96[:, 0:T], AX, ALU.add))
                step(tt(gt_(T), c1[:, 0:T], c2[:, 0:T], ALU.add))
                step(nc.vector.reciprocal(gt_(T), gt_(T)))
                step(tt(c1[:, 0:T], c1[:, 0:T], gt_(T), ALU.mult))
                step(tt(c2[:, 0:T], c2[:, 0:T], gt_(T), ALU.mult))
                dve.wait_ge(ranks_done, l + 1)
                step(nc.vector.tensor_copy(cnt, ps[6][:, 0:NE]))
                step(ts_(ext, cnt, float(P) + 0.5, None, ALU.is_ge))
                for j in range(2, T):
                    step(nc.vector.scalar_tensor_tensor(out=ext, in0=cnt, scalar=float(P) * j + 0.5, in1=ext, op0=ALU.is_ge, op1=ALU.add))
                step(nc.vector.tensor_copy(incl, ext))
                x, y = incl, t16
                for dl in (1, 2, 4, 8):
                    step(nc.vector.tensor_copy(y[:, 0:dl], x[:, 0:dl]))
                    step(tt(y[:, dl:NE], x[:, dl:NE], x[:, 0:NE - dl], ALU.add))
                    x, y = y, x
                step(tt(ovb, x, ext, ALU.subtract))
                step(tt(big, incl.unsqueeze(1).to_broadcast([P, MAX_EXTRA, NE]),
                        C("idx")[:, 0:MAX_EXTRA].unsqueeze(2).to_broadcast([P, MAX_EXTRA, NE]), ALU.is_le))
                step(nc.vector.tensor_copy(tab[:, 0:NE], C("idx")))
                step(nc.vector.tensor_reduce(tab[:, NE:NE + MAX_EXTRA], big, AX, ALU.add))
                step(ts_(tab[:, NE:NE + MAX_EXTRA], tab[:, NE:NE + MAX_EXTRA], float(NE - 1), None, ALU.min))
                step(nc.vector.tensor_copy(tab[:, 28:31], C("idx")[:, 0:3]))
                step(ts_(tab[:, 31:32], incl[:, NE - 1:NE], float(NE), None, ALU.add))
                step(nc.vector.tensor_copy(table_i[:], tab))
                step(ts_(ovb, ovb, float(NE - 1), float(P), ALU.add, ALU.mult))
                step(tt(ovb, ovb, C("e128"), ALU.subtract))
                step(nc.vector.tensor_copy(fl(slot), ps[5][:, 0:T * NE]))
                step(ts_(fl(t96), fl(slot), float(P) - 0.5, None, ALU.is_ge))
                step(tt(t96[:, 0:T], t96[:, 0:T], bc(ovb), ALU.mult))
                step(tt(fl(slot), fl(slot), fl(t96), ALU.add))
                step(tt(slot[:, 0:T], slot[:, 0:T], bc(C("e128")), ALU.add))
                for c, s in enumerate((s1, s2)):
                    step(tt(fl(t96), fl(slot), fl(s), ALU.mult))
                    step(nc.vector.tensor_reduce(slotf[:, 0:T, c], t96[:, 0:T], AX, ALU.add))
                nc.vector.tensor_copy(slot_idx[:, 0:2 * T], slotf[:, 0:T].rearrange("p a b -> p (a b)")).then_inc(table_ready, 1)

            def gt_(T):
                return gt[:, 0:2].rearrange("p a b -> p (a b)")[:, 0:T]

            def experts(l):
                s = L[l]
                T = NT if l == 0 else NL
                prepare_rows(f"ffn{l}", True)
                norms(f"ffn{l}")
                route(l)
                barrier(dve)
                nblk = dve.value_load(table_i[0:1, 31:32], min_val=NE, max_val=NE + MAX_EXTRA)

                def copy_xT():
                    return nc.vector.tensor_copy(xT[:, 4:8, :], ps[1][:].rearrange("p (k n) -> p k n", k=4))

                dve.wait_ge(s["x_turned"], 1)
                copy_xT().then_inc(s["xT_dve"], 1)
                with dve.Fori(0, nblk) as i:
                    dve.wait_ge(s["sil_ready"], i + 1)
                    dve.wait_ge(s["up_done"], i + 1)
                    nc.vector.tensor_tensor(hid, sil, ps[3][:], ALU.mult).then_inc(s["hid_ready"], 1)
                    dve.wait_ge(s["x_turned"], i + 2)
                    copy_xT().then_inc(s["xT_dve"], 1)
                    dve.wait_ge(s["down_done"], i + 1)
                    nc.vector.tensor_copy(ysb[:, 512:1024], ps[6][:]).then_inc(s["y1_ready"], 1)
                for t in range(T):
                    m = t + (0 if l == 0 else NT)
                    base = 0 if l == 0 else 3 * 32
                    dve.wait_ge(gathered[t % 2], base + 32 * (t // 2 + 1))
                    ya, yb = comb[:, 2 * (t % 2)], comb[:, 2 * (t % 2) + 1]
                    grow = rows[:, 4 if t < NL else 5]
                    step(nc.vector.tensor_scalar(ya, ya, c1[:, t:t + 1], None, ALU.mult))
                    step(nc.vector.scalar_tensor_tensor(out=ya, in0=yb, scalar=c2[:, t:t + 1], in1=ya, op0=ALU.mult, op1=ALU.add))
                    step(nc.vector.tensor_tensor(ya, ya, grow, ALU.mult))
                    nc.vector.tensor_tensor(X[:, t], X[:, t], ya, ALU.add).then_inc(combined, 1)
                    dve.wait_ge(combined, m + 1)
                barrier(dve)

            dve.wait_ge(x_in, 16 * NT)
            prepare_rows("mix0", True)
            norms("mix0")
            barrier(dve)
            for m in range(3 * NT):
                n, t = divmod(m, NT)
                z = ps[m % 2]
                nh = 8 if n < 2 else 4
                w = nh * HD
                dve.wait_ge(qkv_product, m + 1)
                if m >= 2:
                    dve.wait_ge(qkv_turned, m - 1)
                dst = zb[:, m % 2]
                hv = lambda v: v[:, 0:w].rearrange("p (h d) -> p h d", h=nh)
                pv = (lambda v: v[:, 0:w].rearrange("p (a c d) -> p a c d", a=2, c=4)) if n < 2 else (lambda v: hv(v))
                dv = (lambda v: v[:, 0:w].rearrange("p (c a d) -> p a c d", a=2, c=4)) if n < 2 else (lambda v: hv(v))
                if n == 2:
                    step(nc.vector.tensor_copy(V[:, t, :], z[:, 256:512]))
                if t < NL:
                    cos, sin = C("cos")[:, t * HD:(t + 1) * HD], C("sin")[:, t * HD:(t + 1) * HD]
                    step(nc.vector.tensor_tensor(hv(rope_a), hv(z[:]), cos.unsqueeze(1).to_broadcast([P, nh, HD]), ALU.mult))
                    q4 = lambda v: v[:, 0:w].rearrange("p (h a f d) -> p h a f d", h=nh, a=2, f=2)
                    s4 = sin.rearrange("p (a f d) -> p a f d", a=2, f=2)
                    for f in range(2):
                        for ax in range(2):
                            step(nc.vector.tensor_tensor(q4(rope_b)[:, :, ax, f, :], q4(z[:])[:, :, ax, 1 - f, :],
                                                         s4[:, ax, f, :].unsqueeze(1).to_broadcast([P, nh, 16]), ALU.mult))
                    nc.vector.tensor_tensor(dv(dst), pv(rope_a), pv(rope_b), ALU.add).then_inc(z_ready, 1)
                else:
                    nc.vector.tensor_copy(dv(dst), pv(z[:])).then_inc(z_ready, 1)
                dve.wait_ge(z_ready, m + 1)
            dve.wait_ge(small_loaded, SMALL["sinks"])
            step(nc.vector.tensor_scalar(sinkrow[:, HEADS:2 * HEADS], sinkrow[:, 0:HEADS], -1.0, None, ALU.mult))
            barrier(dve)

            U = NT * HEADS
            for u in range(U + 2):
                t, h = divmod(u, HEADS)
                if u < U:
                    st, hi = att[:, (u // 8) % 2], h % 8
                    dve.wait_ge(scores_done, u + 1)
                    na = 384 if t < NL else 256
                    if hi == 0 and u >= 16:
                        dve.wait_ge(o_ready, u // 8 - 1)
                    step(nc.vector.tensor_reduce(st[:, hi:hi + 1], ps[u % 2][:, 0:na], AX, ALU.max))
                    top = st[:, hi:hi + 1]
                    if t < NL:
                        nb = 256 if 0 < t < NL - 1 else 128
                        win = C("win")[:, 0:256] if nb == 256 else (C("win")[:, 128:256] if t == 0 else C("win")[:, 0:128])
                        if u >= 2:
                            dve.wait_ge(pb_turned, u - 1)
                        step(nc.vector.tensor_tensor_reduce(out=prob[:, u % 2, 384:384 + nb], in0=ps[2 + u % 2][:, 0:nb], in1=win,
                                                            scale=1.0, scalar=top, op0=ALU.add, op1=ALU.max,
                                                            accum_out=st[:, 40 + hi:41 + hi]))
                        top = st[:, 40 + hi:41 + hi]
                    nc.vector.tensor_scalar(st[:, 8 + hi:9 + hi], top, -(HD ** -0.5), sinkrow[:, HEADS + h:HEADS + h + 1],
                                            ALU.mult, ALU.min).then_inc(shift_ready, 1)
                    dve.wait_ge(shift_ready, u + 1)
                    if hi == 7:
                        nc.vector.tensor_tensor(st[:, 32:40], st[:, 8:16], sinkrow[:, h - 7:h + 1], ALU.add).then_inc(sinkarg_ready, 1)
                if 1 <= u <= U and (u - 1) // HEADS < NL:
                    v = u - 1
                    tv = v // HEADS
                    nb = 256 if 0 < tv < NL - 1 else 128
                    dve.wait_ge(pb_turned, v + 1)
                    if v >= 2:
                        dve.wait_ge(pv_done, v - 1)
                    nc.vector.tensor_copy(probT[:, v % 2, 384:384 + nb], ps[5][:, 0:nb]).then_inc(pb_copied, 1)
                if u >= 2 and (u - 2) % 8 == 7:
                    hh = (u - 2) // 8
                    tv = hh // 2
                    sv = att[:, hh % 2]
                    dve.wait_ge(probs_ready, 8 * hh + 8)
                    dve.wait_ge(sinkexp_ready, hh + 1)
                    step(nc.vector.tensor_tensor(sv[:, 32:40], sv[:, 32:40], sv[:, 16:24], ALU.add))
                    if tv < NL:
                        step(nc.vector.tensor_tensor(sv[:, 32:40], sv[:, 32:40], sv[:, 24:32], ALU.add))
                    step(nc.vector.reciprocal(sv[:, 48:56], sv[:, 32:40]))
                    dve.wait_ge(pv_done, 8 * hh + 8)
                    nc.vector.tensor_tensor(o_tok[:, tv, (hh % 2) * 512:(hh % 2 + 1) * 512].rearrange("p (h d) -> p h d", h=8),
                                            ps[6 + hh % 2][:].rearrange("p (h d) -> p h d", h=8),
                                            sv[:, 48:56].unsqueeze(2).to_broadcast([P, 8, HD]), ALU.mult).then_inc(o_ready, 1)
            barrier(dve)
            out_project(0, NT, lambda t: rows[:, 4 if t < NL else 5], wo_tmp)
            barrier(dve)
            experts(0)
            prepare_rows("mix1", False)
            norms("mix1")
            barrier(dve)
            nc.vector.memset(aT[0:32], 1.0).then_inc(ones_row, 1)
            for n in range(2 * NT):
                t, d = divmod(n, 2)
                l1 = la[:, t, d, :]
                dve.wait_ge(ln_ready, n + 1)
                nc.vector.scalar_tensor_tensor(out=l1, in0=ps[4 + n % 2][:], scalar=0.0, in1=l1, op0=ALU.min,
                                               op1=ALU.subtract).then_inc(la_ready, 1)
            dve.wait_ge(small_loaded, SMALL["gla"])
            for m, (n, t) in enumerate(gla_steps):
                z = ps[6 + m % 2][:]
                if n >= 4:
                    dve.wait_ge(silu_g, m - gla_last[3] + 1)
                    g2 = G[:, t, (n - 4) * 512:(n - 3) * 512].rearrange("p (h v) -> p h v", h=2)
                    nc.vector.tensor_tensor(g2, g2, gnrow.unsqueeze(1).to_broadcast([P, 2, GV]), ALU.mult).then_inc(gla_evac, 1)
                    continue
                dve.wait_ge(gla_product, m + 1)
                if n == 0:
                    if m >= 2:
                        dve.wait_ge(gla_turned, m - 1)
                    ins = nc.vector.tensor_scalar(zq[:, m % 2], z, GK ** -0.5, None, ALU.mult)
                elif n == 1:
                    ins = nc.vector.tensor_copy(ktok[:, t], z)
                else:
                    ins = nc.vector.tensor_copy(Vg[:, t, (n - 2) * 512:(n - 1) * 512], z)
                ins.then_inc(gla_evac, 1)
            barrier(dve)
            barrier(dve)
            for u in range(2 * GH):
                h, d = divmod(u, 2)
                dve.wait_ge(b_copied, u + 1)
                refs = bT.rearrange("p (n w) -> p n w", w=SUB)[:, :, SUB // 2]
                b4 = bT.rearrange("p (t s) -> p t s", t=NL)
                refs4 = refs.rearrange("p (t i) -> p t i", t=NL)
                if u >= 1:
                    dve.wait_ge(s_done, u)
                step(nc.vector.tensor_tensor(qp.rearrange("p (n w) -> p n w", w=SUB), bT.rearrange("p (n w) -> p n w", w=SUB),
                                             refs.unsqueeze(2).to_broadcast([P, NL * 4, SUB]), ALU.subtract))
                for i in range(4):
                    k0, k1 = (0, SUB * (i + 1)) if d == 0 else (SUB * i, P)
                    ins = nc.vector.tensor_tensor(kp[d][:, :, i, k0:k1], refs4[:, :, i:i + 1].to_broadcast([P, NL, k1 - k0]),
                                                  b4[:, :, k0:k1], ALU.subtract)
                    if i < 3:
                        step(ins)
                ins.then_inc(args_ready, 1)
                dve.wait_ge(tails_exp, u + 1)
                nc.vector.tensor_tensor(khat, khat, ktok[:, :, h * GK:(h + 1) * GK], ALU.mult).then_inc(khat_ready, 1)
                dve.wait_ge(exps_ready, u + 1)
                step(nc.vector.tensor_tensor(qp, qp, qTg[:, h], ALU.mult))
                step(nc.vector.tensor_tensor(qh[d], qh[d], qTg[:, h], ALU.mult))
                kh = kTg[:, h].rearrange("p (t s) -> p t s", t=NL)
                for i in range(4):
                    k0, k1 = (0, SUB * (i + 1)) if d == 0 else (SUB * i, P)
                    ins = nc.vector.tensor_tensor(kp[d][:, :, i, k0:k1], kp[d][:, :, i, k0:k1], kh[:, :, k0:k1], ALU.mult)
                    if i < 3:
                        step(ins)
                ins.then_inc(kq_ready, 1)
                order = [4, 5, 0, 1, 2] if d == 0 else [5, 4, 3, 2, 1]
                into = [None, 0, 1, 2, 3] if d == 0 else [None, 3, 2, 1, 0]
                for n, t in enumerate(order):
                    k = 5 * u + n
                    dst = S_tmp if n == 0 else S[d][:, into[n], :]
                    dve.wait_ge(p_done, k + 1)
                    if n == 0:
                        ins = nc.vector.tensor_copy(dst, ps[4 + k % 2][:, 0:GV])
                    else:
                        prev = S_tmp if n == 1 else S[d][:, into[n - 1], :]
                        ins = nc.vector.scalar_tensor_tensor(out=dst, in0=prev, scalar=dec[:, t:t + 1], in1=ps[4 + k % 2][:, 0:GV],
                                                             op0=ALU.mult, op1=ALU.add)
                    ins.then_inc(state_ready, 1)
                    dve.wait_ge(state_ready, k + 1)
                dve.wait_ge(s_done, u + 1)
                mask = C("mask_f") if d == 0 else C("mask_b")
                nc.vector.tensor_tensor(scT[d], ps[3][:].rearrange("p (t s) -> p t s", t=NL),
                                        mask.unsqueeze(1).to_broadcast([P, NL, P]), ALU.mult).then_inc(s_masked, 1)
                if d == 1:
                    for t in range(NL):
                        k = h * NL + t
                        dve.wait_ge(og_rstd, k + 1)
                        g = G[:, t, h * GV:(h + 1) * GV]
                        nc.vector.scalar_tensor_tensor(out=g, in0=ps[6 + k % 2][:, 0:GV], scalar=rsg[:, k % 8:k % 8 + 1], in1=g,
                                                       op0=ALU.mult, op1=ALU.mult).then_inc(og_ready, 1)
            barrier(dve)
            dve.wait_ge(small_loaded, SMALL["grow1"])
            out_project(1, NL, lambda t: grow1, wo_tmp1)
            barrier(dve)
            experts(1)
            dve.wait_ge(rows_loaded, 16 * (rowcount[0] + 1))
            norms("final")


_INS = ["x", "ctx", "ada_w", "ada_b", "norm_mix_g", "norm_ffn_g", "final_g", "attn_w_qkv", "attn_w_o", "attn_sinks",
        "gla_w_in", "gla_norm_g", "gla_w_o", "router_w", "router_b", "moe_w_gate", "moe_w_up", "moe_w_down"]


def kernel(**inputs):
    import concourse.bacc as bacc
    from concourse.bass_utils import run_bass_kernel_spmd as run

    nc = bacc.Bacc("TRN2", target_bir_lowering=False, num_devices=1)
    arrays = {k: np.ascontiguousarray(inputs[k]) for k in _INS}
    both = np.stack([np.asarray(inputs["c"])[0], np.asarray(inputs["c_ctx"])])
    arrays["cT"] = np.ascontiguousarray(both.reshape(2, KC, P).transpose(2, 1, 0))
    arrays["wa1"] = np.ascontiguousarray(np.asarray(inputs["gla_w_a1"])[0].reshape(2, KC, P, RANK).transpose(2, 1, 0, 3).reshape(P, KC, 2 * RANK))
    arrays["a2b"] = np.ascontiguousarray(np.concatenate([np.asarray(inputs["gla_w_a2"])[0], np.asarray(inputs["gla_b_a"])[0][:, None]], 1).transpose(1, 0, 2))
    arrays["const"] = constants()[0]
    aps = {k: nc.dram_tensor(f"in_{k}", v.shape, F32, kind="ExternalInput").ap() for k, v in arrays.items()}
    out = nc.dram_tensor("out", (SEQ, D), F32, kind="ExternalOutput").ap()
    build(nc, aps, out)
    r = run(nc, [{f"in_{k}": v for k, v in arrays.items()}], core_ids=[0])
    return np.asarray(r.results[0]["out"]).reshape(1, SEQ, D)
```

```python
from contextlib import ExitStack

import numpy as np
import concourse.bass as bass
from concourse import mybir
from concourse.alu_op_type import AluOpType as ALU

ACT = mybir.ActivationFunctionType
F32 = mybir.dt.float32
I32 = mybir.dt.int32
U32 = mybir.dt.uint32
AX = mybir.AxisListType.X

P = 128
D = 1024
KC = D // P
SEQ, CTX = 512, 256
NL, NX = SEQ // P, CTX // P
NT = NL + NX
GRID_W = 64
EPS = 1e-6
NEG = -1e30
PW = 512
RING = 3
HEADS, HD = 16, 64
HQ = 4
GH, GK, GV = 4, 128, 256
RANK = 16
SUB = 32
NE, NG, EPG = 16, 4, 4
DE = 512
FC = DE // P
MAX_EXTRA = 12
NBLK = NE + MAX_EXTRA + 1


def constants():
    i, j = np.arange(P)[:, None], np.arange(P)[None, :]
    f = np.float32
    inv = (10000.0 ** (-np.arange(16, dtype=f) / f(16))).astype(f)
    pos = np.arange(SEQ)
    ang = np.stack([(pos // GRID_W).astype(f)[:, None] * inv, (pos % GRID_W).astype(f)[:, None] * inv], 1)
    c, s = np.cos(ang), np.sin(ang)
    cos = np.stack([c, c], 2).reshape(NL, P, HD).transpose(1, 0, 2).reshape(P, -1)
    sin = np.stack([-s, s], 2).reshape(NL, P, HD).transpose(1, 0, 2).reshape(P, -1)
    row = lambda v: np.tile(np.asarray(v, f)[None, :], (P, 1))
    parts = {
        "ident": (i == j), "ones": np.ones((P, P)), "before": (i < j),
        "mask_f": (i <= j), "mask_b": (i >= j),
        "cum_f": (i <= j) / 16.0, "cum_b": (i >= j) / 16.0,
        "tail_f": (i > j) / 16.0, "tail_b": (i < j) / 16.0, "sixteenth": np.full((P, 1), 1 / 16.0),
        "win": np.concatenate([np.where(j >= i, 0, NEG), np.where(j <= i, 0, NEG)], 1),
        "cos": cos, "sin": sin, "neghalf": np.full((P, 1), -0.5), "one": np.ones((P, 1)),
        "fold": (i % 32 == np.arange(2)[None, :]), "wins": row([3, 2, 1, 0] * 4), "e128": row(np.arange(NE) * 128), "idx": row(np.arange(16)),
    }
    off, out, n = {}, [], 0
    for k, v in parts.items():
        v = np.asarray(v, f)
        off[k] = (n, n + v.shape[1])
        n += v.shape[1]
        out.append(v)
    return np.ascontiguousarray(np.concatenate(out, 1)), off


class Region:

    def __init__(self, arena, at, end):
        self.arena, self.at, self.end = arena, at, end

    def take(self, *shape):
        n = int(np.prod(shape))
        ap = self.arena[:, self.at:self.at + n]
        self.at += n
        assert self.at <= self.end, (self.at, self.end)
        if len(shape) == 2:
            ap = ap.rearrange("p (a b) -> p a b", a=shape[0])
        elif len(shape) == 3:
            ap = ap.rearrange("p (a b c) -> p a b c", a=shape[0], b=shape[1])
        return ap


class Steps:

    def __init__(self, eng, sem):
        self.eng, self.sem, self.n, self.base = eng, sem, 0, None

    def __call__(self, ins):
        ins.then_inc(self.sem, 1)
        self.n += 1
        self.eng.wait_ge(self.sem, self.n if self.base is None else self.base + self.n)


def build(nc, a, out):
    with ExitStack() as ctx:
        sem = lambda name: ctx.enter_context(nc.semaphore(name))
        const_np, coff = constants()
        ncon = const_np.shape[1]
        ARENA = 53100
        arena = ctx.enter_context(nc.sbuf_tensor("arena", [P, ARENA], F32))
        slot_idx = ctx.enter_context(nc.sbuf_tensor("slot_idx", [P, NT * 2], U32))
        table_i = ctx.enter_context(nc.sbuf_tensor("table_i", [P, 32], I32))
        ps = [ctx.enter_context(nc.psum_tensor(f"bank{b}", [P, 512], F32)) for b in range(8)]

        mods = nc.dram_tensor("mods", [2, 2 * 6 * D], F32, kind="Internal").ap()
        xbuf = nc.dram_tensor("xbuf", [NBLK * P, D], F32, kind="Internal").ap()
        ybuf = nc.dram_tensor("ybuf", [NBLK * P, D], F32, kind="Internal").ap()

        ADA0, ADA = 6, 24
        fixed = Region(arena, 0, ARENA)
        ring = fixed.take(RING, KC * PW)
        X = fixed.take(NT, D)
        rows0 = fixed.at
        rows = fixed.take(6, D)
        hT0 = fixed.at
        hT = fixed.take(KC, NT * P)
        con = fixed.take(ncon)
        cT = fixed.take(KC, 2)
        csil = fixed.take(KC, 2)
        c32 = fixed.take(KC, 32)
        stat = fixed.take(256)
        R0 = fixed.at
        C = lambda k: con[:, coff[k][0]:coff[k][1]]
        ident, ones = C("ident"), C("ones")
        region = lambda at=R0, end=ARENA: Region(arena, at, end)
        ss, ms, rstd = stat[:, 0:32], stat[:, 32:64], stat[:, 64:96]

        r = region()
        hbuf = r.take(2, D)
        junk = r.take(D)
        zb, rope_a, rope_b = r.take(2, 512), r.take(512), r.take(512)
        first_at = r.at
        qT = r.take(KC, NT * P)
        first = region(first_at, r.at)
        first_bias, first_out = first.take(ADA0 * PW), first.take(ADA0 * PW)
        kT = r.take(2 * 2, NT * P)
        V = r.take(NT, 256)
        ada_at = r.at
        prob, probT = r.take(2, 640), r.take(2, 640)
        ada = region(ada_at, r.at)
        ada_sum, ada_bias, ada_out = ada.take(PW), ada.take(2, PW), ada.take(2, PW)
        att = r.take(2, 64)
        sinkrow = r.take(32)
        o_tok = region(hT0, R0).take(NT, D)
        oT = qT
        wo_tmp = r.take(512)
        r = region()
        H = r.take(NT, D)
        xg = r.take(D)
        xT = r.take(KC, P)
        sil, hid, hidT, ysb = r.take(DE), r.take(DE), r.take(FC, P), r.take(D)
        comb = r.take(4, D)
        rw = r.take(KC, NE)
        rt = Region(arena, r.at, r.at + 96 * 10 + 200)
        sc, sel, posn, s1, s2, M, t96, t96b, slot = [rt.take(NT, NE) for _ in range(9)]
        gs, gpos, g1, gt = [rt.take(NT, NG) for _ in range(4)]
        c1, c2, slotf = rt.take(NT), rt.take(NT), rt.take(NT, 2)
        r.at = rt.at
        cnt, ext, incl, t16, ovb, tab = [r.take(NE) for _ in range(5)] + [r.take(32)]
        big = r.take(MAX_EXTRA, NE)
        rbrow = r.take(NE)
        r = region()
        hb_at = r.at
        r.take(2, D)
        a2b = region(hb_at + 1024).take(2, 512)
        ktok, kTg, qTg, Vg, G = r.take(NT, 512), r.take(GH, SEQ), r.take(GH, SEQ), r.take(NT, D), r.take(NL, D)
        zq = region(r.at - 2 * D).take(2, 512)
        xc_at = RING * KC * PW + NL * D
        xc = region(xc_at, xc_at + NX * D)
        aT, wa1, gnrow = xc.take(NT * P), xc.take(KC, 2 * RANK), xc.take(GV)
        la = region(rows0, hT0).take(NT, 2, 512)
        r2 = region(hT0, hT0 + 6144)
        kp = [r2.take(4, 4, P) for _ in range(2)]
        bT0, qh0 = r2.take(SEQ), r2.take(SEQ)
        scT0, scT1 = r2.take(NL, P), r2.take(NL, P)
        r3 = region(hb_at, hb_at + 2048)
        qh1, qp0 = r3.take(SEQ), r3.take(SEQ)
        khat0 = r3.take(NT, P)
        S_tmp = r3.take(GV)
        r4 = Region(arena, xc_at, xc_at + 2048)
        S = [r4.take(NL, GV) for _ in range(2)]
        slot_at = (ADA + 3 + 2 + 3 + 6 + 2) % RING * KC * PW
        r6 = region(slot_at, slot_at + KC * PW)
        bT, qp, khat = [bT0, r6.take(SEQ)], [qp0, r6.take(SEQ)], [khat0, r6.take(NT, P)]
        qh, scT = [qh0, qh1], [scT0, scT1]
        r5 = region(R0 + 9216, R0 + 15360)
        oTg, grow1, wo_tmp1 = r5.take(KC, SEQ), r5.take(D), r5.take(512)
        gain = arena[:, R0:R0 + D]
        junks = {"mix0": junk, "mix1": junk, "ffn0": probT.rearrange("p a b -> p (a b)")[:, 0:D],
                 "ffn1": arena[:, R0 + 5120:R0 + 5120 + D], "final": xg}
        dec = [stat[:, 96:104], stat[:, 136:144]]
        ssg = stat[:, 104:112]
        msg = stat[:, 112:120]
        rsg = stat[:, 120:128]

        def ring_panel(slot):
            return ring[:, slot].rearrange("p (k n) -> p k n", k=KC)

        def panel(j):
            return ring_panel(j % RING)

        def down_panel(j):
            return ring[:, j % RING].rearrange("p (f n) -> p f n", f=FC)

        place = {}
        arrivals = []

        def put(name, slot):
            place[name] = (slot, 1 + sum(place[k][0] == slot for k in arrivals))
            arrivals.append(name)

        for j in range(ADA0):
            put(("ada", j), j % RING)
        for n in range(3):
            put(("qkv", n), n)
            for j in range(6):
                put(("ada", ADA0 + 6 * n + j), (n + 1 + j % 2) % RING)
        J_WO0 = ADA + 3
        J_M0 = J_WO0 + 2
        J_GLA = J_M0 + 3
        J_WO1 = J_GLA + 6
        J_M1 = J_WO1 + 2

        consts_loaded, c_loaded, c_silu = sem("consts_loaded"), sem("c_loaded"), sem("c_silu")
        x_in, zeroed, zero_ready = sem("x_in"), sem("zeroed"), sem("zero_ready")
        panel_loaded = [sem(f"panel_loaded{s}") for s in range(RING)]
        ada_partial, ada_copied, mods_product, mods_added = sem("ada_partial"), sem("ada_copied"), sem("mods_product"), sem("mods_added")
        mods_stored, bias_loaded = [sem("mods_stored0"), sem("mods_stored1")], [sem("bias_loaded0"), sem("bias_loaded1")]
        rows_loaded, gates_loaded, small_loaded = sem("rows_loaded"), sem("gates_loaded"), sem("small_loaded")
        grow_loaded = sem("grow_loaded")
        first_loaded, first_stored = sem("first_loaded"), sem("first_stored")
        phase_end = sem("phase_end")
        sumsq_ready, rstd_ready, normed, h_turned, hT_copied = sem("sumsq_ready"), sem("rstd_ready"), sem("normed"), sem("h_turned"), sem("hT_copied")
        act_steps, dve_steps, pool_steps = sem("act_steps"), sem("dve_steps"), sem("pool_steps")
        qkv_product, z_ready, qkv_turned, qkvT_copied = sem("qkv_product"), sem("z_ready"), sem("qkv_turned"), sem("qkvT_copied")
        scores_done, shift_ready, probs_ready = sem("scores_done"), sem("shift_ready"), sem("probs_ready")
        pa_turned, pb_turned, pa_copied, pb_copied = sem("pa_turned"), sem("pb_turned"), sem("pa_copied"), sem("pb_copied")
        pv_done, sinkarg_ready, sinkexp_ready, o_ready = sem("pv_done"), sem("sinkarg_ready"), sem("sinkexp_ready"), sem("o_ready")
        wo_product, wo_added = [sem("wo_product0"), sem("wo_product1")], [sem("wo_added0"), sem("wo_added1")]
        logits_done, gates_exp, picks_ready, ranks_done = sem("logits_done"), sem("gates_exp"), sem("picks_ready"), sem("ranks_done")
        table_ready, scattered = sem("table_ready"), sem("scattered")
        L = [{n: sem(f"{n}{l}") for n in (
            "x_loaded", "x_turned", "xT_act", "xT_dve", "gate_done", "up_done", "sil_ready", "hid_ready",
            "hid_turned", "hidT_ready", "down_done", "y0_ready", "y1_ready", "y_stored")} for l in range(2)]
        gathered = [sem("gathered_a"), sem("gathered_b")]
        combined = sem("combined")
        a_product, a_copied, z_product, ln_ready, la_ready = sem("a_product"), sem("a_copied"), sem("z_product"), sem("ln_ready"), sem("la_ready")
        gla_product, gla_evac, gla_turned, glaT_copied, silu_g = sem("gla_product"), sem("gla_evac"), sem("gla_turned"), sem("glaT_copied"), sem("silu_g")
        b_done, b_copied, tails_done, tails_exp = sem("b_done"), sem("b_copied"), sem("tails_done"), sem("tails_exp")
        args_ready, exps_ready, kq_ready, khat_ready = sem("args_ready"), sem("exps_ready"), sem("kq_ready"), sem("khat_ready")
        qh_exp, qh_ready = sem("qh_exp"), sem("qh_ready")
        s_done, s_masked, p_done, state_ready, og_done = sem("s_done"), sem("s_masked"), sem("p_done"), sem("state_ready"), sem("og_done")
        og_sq, og_rstd, og_ready = sem("og_sq"), sem("og_rstd"), sem("og_ready")
        out_stored, ones_row = sem("out_stored"), sem("ones_row")
        SMALL = {"sinks": 16, "router": (48, 128), "gla": 96}

        NORM = {"mix0": (list(range(NT)), 0), "ffn0": (list(range(NT)), 6), "mix1": (list(range(NT)), 12),
                "ffn1": (list(range(NL)), 18), "final": (list(range(NL)), 22)}
        TURN = {"mix0": 0, "wo0": 6, "ffn0": 12, "mix1": 18, "wo1": 24, "ffn1": 28}
        MODULE = {"mix0": (0, 0, "norm_mix_g"), "ffn0": (0, 3, "norm_ffn_g"), "mix1": (1, 0, "norm_mix_g"), "ffn1": (1, 3, "norm_ffn_g")}
        ROWSEQ = ["mix0", "ffn0", "mix1", "ffn1", "final"]
        gla_steps = ([(0, t) for t in range(NL)] + [(1, t) for t in range(NT)] + [(n, t) for n in (2, 3) for t in range(NT)]
                     + [(n, t) for n in (4, 5) for t in range(NL)])
        gla_last = [max(m for m, (n, _) in enumerate(gla_steps) if n == k) + 1 for k in range(6)]
        turn_of = {m: i for i, m in enumerate([m for m, (n, t) in enumerate(gla_steps) if n < 2 and t < NL])}

        Z0 = max(turn_of) + 4
        phases = {}

        def barrier(eng):
            phases[eng.engine] = phases.get(eng.engine, 0) + 1
            eng.drain().then_inc(phase_end, 1)
            eng.wait_ge(phase_end, 4 * phases[eng.engine])

        def wait_panel(eng, j, extra=None):
            n = 16 * (j // RING + 1)
            eng.wait_ge(panel_loaded[j % RING], n if extra is None else extra + n)

        block = ctx.enter_context(nc.Block())

        @block.sync
        def _(sp):
            sp.dma_start(con, a["const"]).then_inc(consts_loaded, 16)
            sp.dma_start(cT, a["cT"]).then_inc(c_loaded, 16)

            def load(j, src, k=KC):
                dst = panel(j) if k == KC else down_panel(j)
                sp.dma_start(dst, src).then_inc(panel_loaded[j % RING], 16)

            def cols(w, n):
                return w[:, n * PW:(n + 1) * PW].rearrange("(k p) n -> p k n", p=P)

            released = {}
            for kind, j in arrivals:
                slot = place[kind, j][0]
                if (kind, j) == ("qkv", 0):
                    sp.wait_ge(rows_loaded, 16 * 5)
                if slot in released:
                    sp.wait_ge(*released[slot])
                w = a["ada_w"][j // 12] if kind == "ada" else a["attn_w_qkv"][0]
                sp.dma_start(ring_panel(slot), cols(w, j % 12)).then_inc(panel_loaded[slot], 16)
                released[slot] = (ada_partial, j + 1) if kind == "ada" else (qkv_product, NT * (j + 1))
            for n in range(2):
                sp.wait_ge(*released[n])
                load(J_WO0 + n, cols(a["attn_w_o"][0], n))

            sp.wait_ge(zero_ready, 1)
            sp.wait_ge(scores_done, 1)
            for buf in (xbuf, ybuf):
                sp.dma_start(buf.rearrange("(b p) n -> p b n", p=P),
                             rows[:, 0:1, :].to_broadcast([P, NBLK, D])).then_inc(zeroed, 16)

            def experts(l, j0, first_waits, extra):
                s = L[l]
                wg = a["moe_w_gate"][l].rearrange("e (k p) n -> e p k n", p=P)
                wu = a["moe_w_up"][l].rearrange("e (k p) n -> e p k n", p=P)
                wd = a["moe_w_down"][l].rearrange("e (f p) n -> e p f n", p=P)
                for n, w in enumerate((wg, wu, wd)):
                    first_waits[n]()
                    load(j0 + n, w[0], FC if n == 2 else KC)
                sp.wait_ge(table_ready, l + 1)
                nblk = sp.value_load(table_i[0:1, 31:32], min_val=NE, max_val=NE + MAX_EXTRA)
                sp.wait_ge(scattered, 16 * 2 * (NT if l == 0 else NT + NL))
                sp.dma_start(xg, xbuf[0:P, :]).then_inc(s["x_loaded"], 16)
                with sp.Fori(1, nblk) as i:
                    e = sp.value_load(table_i[0:1, bass.ds(i, 1)], min_val=0, max_val=NE - 1)
                    sp.wait_ge(s["x_turned"], i)
                    sp.dma_start(xg, xbuf[bass.ds(i * P, P), :]).then_inc(s["x_loaded"], 16)
                    for n, (w, used) in enumerate(((wg, "gate_done"), (wu, "up_done"), (wd, "down_done"))):
                        sp.wait_ge(s[used], i)
                        src = w[bass.ds(e, 1)].rearrange("o p k n -> (o p) k n")
                        load(j0 + n, src, FC if n == 2 else KC)
                sp.wait_ge(s["x_turned"], nblk)
                sp.dma_start(xg, xbuf[bass.ds(nblk * P, P), :]).then_inc(s["x_loaded"], 16)
                return nblk

            n0 = experts(0, J_M0, [lambda: sp.wait_ge(qkv_product, 3 * NT), lambda: sp.wait_ge(wo_product[0], 2 * NT),
                                   lambda: sp.wait_ge(wo_product[0], 2 * NT)], None)
            for n in range(6):
                if n < 3:
                    sp.wait_ge(L[0][("gate_done", "up_done", "down_done")[n]], n0)
                else:
                    sp.wait_ge(gla_product, gla_last[n - 3])
                load(J_GLA + n, cols(a["gla_w_in"][0], n))
            for n in range(2):
                sp.wait_ge(gla_product, gla_last[3 + n])
                load(J_WO1 + n, cols(a["gla_w_o"][0], n))
            experts(1, J_M1, [lambda: sp.wait_ge(og_done, GH * NL), lambda: sp.wait_ge(wo_product[1], 2 * NL),
                              lambda: sp.wait_ge(wo_product[1], 2 * NL)], n0)
            for t in range(NL):
                sp.wait_ge(normed, NORM["final"][1] + t + 1)
                sp.dma_start(out[t * P:(t + 1) * P, :], H[:, t]).then_inc(out_stored, 16)
            sp.wait_ge(out_stored, 16 * NL)

        @block.gpsimd
        def _(pool):
            step = Steps(pool, pool_steps)
            pool.dma_start(first_bias[0:2], a["ada_b"][0:1, 0:ADA0 * PW].to_broadcast([2, ADA0 * PW])).then_inc(first_loaded, 16)
            pool.wait_ge(consts_loaded, 16)
            for t in range(NT):
                src = a["x"][0, t * P:(t + 1) * P, :] if t < NL else a["ctx"][0, (t - NL) * P:(t - NL + 1) * P, :]
                pool.dma_start(X[:, t], src).then_inc(x_in, 16)

            def load_bias(j):
                src = a["ada_b"][j // 12:j // 12 + 1, (j % 12) * PW:(j % 12 + 1) * PW].to_broadcast([2, PW])
                pool.dma_start(ada_bias[0:2, j % 2], src).then_inc(bias_loaded[j % 2], 16)

            def store_mods():
                for j in range(ADA0, ADA):
                    pool.wait_ge(mods_added, j + 1)
                    pool.dma_start(mods[:, j * PW:(j + 1) * PW], ada_out[0:2, j % 2]).then_inc(mods_stored[j % 2], 16)
                    if j + 2 < ADA:
                        load_bias(j + 2)
                for k in range(2):
                    pool.wait_ge(mods_stored[k], 16 * (ADA - ADA0) // 2)

            load_bias(ADA0)
            load_bias(ADA0 + 1)
            pool.wait_ge(mods_added, ADA0)
            pool.dma_start(mods[:, 0:ADA0 * PW], first_out[0:2]).then_inc(first_stored, 16)
            pool.wait_ge(first_stored, 16)

            def row_loads(name):
                l, part, gain_in = MODULE[name]
                for stream in range(2):
                    for n, q in enumerate((part + 1, part)):
                        src = mods[stream:stream + 1, (l * 6 + q) * D:(l * 6 + q + 1) * D]
                        pool.dma_start(rows[:, 2 * stream + n], src.to_broadcast([P, D])).then_inc(rows_loaded, 16)
                pool.dma_start(gain, a[gain_in][l:l + 1, :].to_broadcast([P, D])).then_inc(rows_loaded, 16)

            def gate_loads(name):
                l, part, _ = MODULE[name]
                for stream in range(2):
                    src = mods[stream:stream + 1, (l * 6 + part + 2) * D:(l * 6 + part + 3) * D]
                    pool.dma_start(rows[:, 4 + stream], src.to_broadcast([P, D])).then_inc(gates_loaded, 16)

            def rstd_tile(name, t):
                q = NORM[name][1] + t
                pool.wait_ge(sumsq_ready, q + 1)
                step(nc.gpsimd.tensor_scalar(ms[:, q:q + 1], ss[:, q:q + 1], 1.0 / D, EPS, ALU.mult, ALU.add))
                nc.gpsimd.tensor_tensor(rstd[:, q:q + 1], ms[:, q:q + 1], C("neghalf"), ALU.pow).then_inc(rstd_ready, 1)

            def small(dst, src):
                pool.dma_start(dst, src).then_inc(small_loaded, 16)

            def experts(l):
                T = NT if l == 0 else NL
                pool.wait_ge(h_turned, TURN[f"wo{l}"] + T)
                small(rw, a["router_w"].rearrange("(k p) e -> p k e", p=P))
                small(rbrow, a["router_b"].unsqueeze(0).to_broadcast([P, NE]))
                for t in range(T):
                    rstd_tile(f"ffn{l}", t)
                pool.wait_ge(wo_added[l], 2 * T)
                gate_loads(f"ffn{l}")
                pool.wait_ge(table_ready, l + 1)
                for t in range(T):
                    for c in range(2):
                        pool.indirect_dma_start(
                            out=xbuf[:, :], out_offset=bass.IndirectOffsetOnAxis(ap=slot_idx[:, 2 * t + c:2 * t + c + 1], axis=0),
                            in_=H[:, t], in_offset=None).then_inc(scattered, 16)
                barrier(pool)
                nxt = "mix1" if l == 0 else "final"
                pool.wait_ge(scattered, 16 * 2 * (NT if l == 0 else NT + NL))
                if l == 0:
                    row_loads("mix1")
                else:
                    pool.dma_start(rows[:, 0], a["final_g"].unsqueeze(0).to_broadcast([P, D])).then_inc(rows_loaded, 16)
                barrier(pool)
                nblk = pool.value_load(table_i[0:1, 31:32], min_val=NE, max_val=NE + MAX_EXTRA)
                pool.wait_ge(L[l]["y_stored"], nblk * 16)
                step(nc.gpsimd.tensor_tensor(stat[:, 130:131], C("one"), C("one"), ALU.mult))
                for t in range(T):
                    m = t + (0 if l == 0 else NT)
                    if t >= 2:
                        pool.wait_ge(combined, m - 1)
                    for c in range(2):
                        pool.indirect_dma_start(
                            out=comb[:, 2 * (t % 2) + c], out_offset=None, in_=ybuf[:, :],
                            in_offset=bass.IndirectOffsetOnAxis(ap=slot_idx[:, 2 * t + c:2 * t + c + 1], axis=0)
                        ).then_inc(gathered[t % 2], 16)
                    if t >= 2:
                        rstd_tile(nxt, t - 2)
                rstd_tile(nxt, T - 2)
                rstd_tile(nxt, T - 1)

            barrier(pool)
            row_loads("mix0")
            gate_loads("mix0")
            step(nc.gpsimd.memset(kT, 0.0))
            for t in range(NT):
                rstd_tile("mix0", t)
            barrier(pool)
            store_mods()
            nc.gpsimd.memset(rows[:, 0], 0.0).then_inc(zero_ready, 1)
            small(sinkrow[:, 0:HEADS], a["attn_sinks"].to_broadcast([P, HEADS]))
            barrier(pool)
            barrier(pool)
            pool.wait_ge(zeroed, 16 * 2)
            row_loads("ffn0")
            experts(0)
            pool.wait_ge(normed, NORM["mix1"][1] + NT)
            pool.wait_ge(h_turned, TURN["mix1"] + NT)
            small(wa1, a["wa1"])
            small(a2b, a["a2b"])
            small(gnrow, a["gla_norm_g"].to_broadcast([P, GV]))
            barrier(pool)
            step(nc.gpsimd.memset(kp[0], 0.0))
            step(nc.gpsimd.memset(kp[1], 0.0))
            barrier(pool)
            for n in range(GH * NL):
                pool.wait_ge(og_sq, n + 1)
                step(nc.gpsimd.tensor_scalar(msg[:, n % 8:n % 8 + 1], ssg[:, n % 8:n % 8 + 1], 1.0 / GV, EPS, ALU.mult, ALU.add))
                nc.gpsimd.tensor_tensor(rsg[:, n % 8:n % 8 + 1], msg[:, n % 8:n % 8 + 1], C("neghalf"), ALU.pow).then_inc(og_rstd, 1)
            barrier(pool)
            pool.dma_start(grow1, mods[0:1, (6 + 2) * D:(6 + 3) * D].to_broadcast([P, D])).then_inc(grow_loaded, 16)
            row_loads("ffn1")
            experts(1)

        @block.tensor
        def _(pe):
            def turn_tile(name, src, t, ready=None):
                g = TURN[name] + t
                if ready is not None:
                    pe.wait_ge(ready, NORM[name][1] + t + 1)
                if g >= 2:
                    pe.wait_ge(hT_copied, g - 1)
                for k in range(KC):
                    mm = nc.tensor.transpose(ps[2 * (g % 2) + k // 4][:, (k % 4) * P:(k % 4 + 1) * P],
                                             src[:, k * P:(k + 1) * P], ident)
                mm.then_inc(h_turned, 1)

            def product(bank, lhsT, rhs, n=KC):
                for k in range(n):
                    mm = nc.tensor.matmul(bank, lhsT(k), rhs(k), start=(k == 0), stop=(k == n - 1))
                return mm

            def out_project(l, src, oTx, T, j0, extra):
                for t in range(T):
                    turn_tile(f"wo{l}", src[:, t], t)
                for n in range(2):
                    wait_panel(pe, j0 + n, extra)
                for t in range(T + 2):
                    if t < T:
                        pe.wait_ge(hT_copied, TURN[f"wo{l}"] + t + 1)
                        for n in range(2):
                            m = 2 * t + n
                            if m >= 3:
                                pe.wait_ge(wo_added[l], m - 2)
                            product(ps[4 + m % 3][:], lambda k: oTx[:, k, t * P:(t + 1) * P],
                                    lambda k: panel(j0 + n)[:, k, :]).then_inc(wo_product[l], 1)
                    if 1 <= t <= T:
                        turn_tile(f"ffn{l}", H[:, t - 1], t - 1, normed)
                    if t >= 2:
                        v = t - 2
                        if v == 0:
                            pe.wait_ge(small_loaded, SMALL["router"][l])
                        pe.wait_ge(hT_copied, TURN[f"ffn{l}"] + v + 1)
                        mm = product(ps[7][:, v * NE:(v + 1) * NE], lambda k: hT[:, k, v * P:(v + 1) * P], lambda k: rw[:, k, :])
                mm.then_inc(logits_done, 1)

            def experts(l, j0, extra):
                T = NT if l == 0 else NL
                s = L[l]
                pe.wait_ge(picks_ready, l + 1)
                for t in range(T):
                    for t2 in range(t):
                        nc.tensor.matmul(ps[5][:, t * NE:(t + 1) * NE], ones, M[:, t2], start=(t2 == 0), stop=False)
                    nc.tensor.matmul(ps[5][:, t * NE:(t + 1) * NE], C("before"), M[:, t], start=(t == 0), stop=True)
                mm = product(ps[6][:, 0:NE], lambda t: ones, lambda t: M[:, t], T)
                mm.then_inc(ranks_done, 1)
                barrier(pe)
                nblk = pe.value_load(table_i[0:1, 31:32], min_val=NE, max_val=NE + MAX_EXTRA)
                gp, up, dp = panel(j0), panel(j0 + 1), down_panel(j0 + 2)

                def turn_block():
                    for k in range(KC):
                        mm = nc.tensor.transpose(ps[k // 4][:, (k % 4) * P:(k % 4 + 1) * P], xg[:, k * P:(k + 1) * P], ident)
                    mm.then_inc(s["x_turned"], 1)

                pe.wait_ge(s["x_loaded"], 16)
                turn_block()
                with pe.Fori(0, nblk) as i:
                    i16 = i * 16 if extra is None else i * 16 + extra
                    pe.wait_ge(s["xT_act"], i + 1)
                    pe.wait_ge(s["xT_dve"], i + 1)
                    wait_panel(pe, j0, i16)
                    product(ps[2][:], lambda k: xT[:, k, :], lambda k: gp[:, k, :]).then_inc(s["gate_done"], 1)
                    wait_panel(pe, j0 + 1, i16)
                    product(ps[3][:], lambda k: xT[:, k, :], lambda k: up[:, k, :]).then_inc(s["up_done"], 1)
                    pe.wait_ge(s["x_loaded"], i * 16 + 32)
                    turn_block()
                    pe.wait_ge(s["hid_ready"], i + 1)
                    for f in range(FC):
                        mm = nc.tensor.transpose(ps[4][:, f * P:(f + 1) * P], hid[:, f * P:(f + 1) * P], ident)
                    mm.then_inc(s["hid_turned"], 1)
                    pe.wait_ge(s["hidT_ready"], i + 1)
                    wait_panel(pe, j0 + 2, i16)
                    product(ps[5][:], lambda f: hidT[:, f, :], lambda f: dp[:, f, 0:512], FC)
                    product(ps[6][:], lambda f: hidT[:, f, :], lambda f: dp[:, f, 512:1024], FC).then_inc(s["down_done"], 1)
                barrier(pe)
                return nblk

            pe.wait_ge(consts_loaded, 16)
            pe.wait_ge(c_silu, 3)

            def ada_terms(j):
                slot, n = place["ada", j]
                pe.wait_ge(panel_loaded[slot], 16 * n)
                if j >= 2:
                    pe.wait_ge(ada_copied, j - 1)
                for k in range(KC):
                    q = 32 * (k % 4)
                    mm = nc.tensor.matmul(ps[4 + j % 2][q:q + 32, :], c32[:, k, :], ring_panel(slot)[:, k, :],
                                          start=(k < 4), stop=(k >= 4), skip_group_check=True)
                mm.then_inc(ada_partial, 1)

            def ada_fold(j):
                pe.wait_ge(ada_copied, j + 1)
                if j >= 2:
                    pe.wait_ge(mods_added, j - 1)
                nc.tensor.matmul(ps[6 + j % 2][0:2, :], C("fold"), ada_sum, start=True, stop=True).then_inc(mods_product, 1)

            for j in range(ADA0 + 1):
                if j < ADA0:
                    ada_terms(j)
                if j >= 1:
                    ada_fold(j - 1)
            barrier(pe)
            for t in range(NT):
                turn_tile("mix0", hbuf[:, t % 2], t, normed)
            barrier(pe)

            def turn_z(m):
                n = m // NT
                pe.wait_ge(z_ready, m + 1)
                if m >= 2:
                    pe.wait_ge(qkvT_copied, m - 1)
                for c in range(4 if n < 2 else 2):
                    mm = nc.tensor.transpose(ps[2 + m % 2][:, c * P:(c + 1) * P], zb[:, m % 2, c * P:(c + 1) * P], ident)
                mm.then_inc(qkv_turned, 1)

            for m in range(3 * NT + 1):
                if m < 3 * NT:
                    n, t = divmod(m, NT)
                    slot, ld = place["qkv", n]
                    if t == 0:
                        pe.wait_ge(panel_loaded[slot], 16 * ld)
                    if m >= 2:
                        pe.wait_ge(z_ready, m - 1)
                    product(ps[m % 2][:], lambda k: hT[:, k, t * P:(t + 1) * P], lambda k: ring_panel(slot)[:, k, :]).then_inc(qkv_product, 1)
                    ada_terms(ADA0 + m)
                if m >= 1:
                    turn_z(m - 1)
                    ada_fold(ADA0 + m - 1)
            barrier(pe)

            U = NT * HEADS

            def scores(u):
                t, h = divmod(u, HEADS)
                n, par, c = h // 8, (h % 8) // 4, h % 4
                q = qT[:, n * 4 + c, t * P:(t + 1) * P]
                kk = lambda c0, c1: kT[:, 2 * par + n, c0:c1]
                if u >= 2:
                    pe.wait_ge(probs_ready, u - 1)
                if t < NL:
                    nc.tensor.matmul(ps[u % 2][:, 0:P], q, kk(t * P, (t + 1) * P), start=True, stop=True)
                    nc.tensor.matmul(ps[u % 2][:, P:P + CTX], q, kk(SEQ, SEQ + CTX), start=True, stop=True)
                    b = ps[2 + u % 2]
                    if 0 < t < NL - 1:
                        nc.tensor.matmul(b[:, 0:P], q, kk((t - 1) * P, t * P), start=True, stop=True)
                        mm = nc.tensor.matmul(b[:, P:2 * P], q, kk((t + 1) * P, (t + 2) * P), start=True, stop=True)
                    else:
                        o = t + 1 if t == 0 else t - 1
                        mm = nc.tensor.matmul(b[:, 0:P], q, kk(o * P, (o + 1) * P), start=True, stop=True)
                else:
                    mm = nc.tensor.matmul(ps[u % 2][:, 0:CTX], q, kk(SEQ, SEQ + CTX), start=True, stop=True)
                mm.then_inc(scores_done, 1)

            def turn_probs(u):
                t = u // HEADS
                pe.wait_ge(probs_ready, u + 1)
                if u >= 1:
                    pe.wait_ge(pa_copied, u)
                for c in range(3 if t < NL else 2):
                    mm = nc.tensor.transpose(ps[4][:, c * P:(c + 1) * P], prob[:, u % 2, c * P:(c + 1) * P], ident)
                mm.then_inc(pa_turned, 1)
                if t < NL:
                    if u >= 1:
                        pe.wait_ge(pb_copied, u)
                    for c in range(2 if 0 < t < NL - 1 else 1):
                        mm = nc.tensor.transpose(ps[5][:, c * P:(c + 1) * P], prob[:, u % 2, (3 + c) * P:(4 + c) * P], ident)
                    mm.then_inc(pb_turned, 1)

            def values(u):
                t, h = divmod(u, HEADS)
                hh = u // HQ
                if t < NL:
                    keys = [t, NL, NL + 1] + ([t - 1, t + 1] if 0 < t < NL - 1 else [t + 1 if t == 0 else t - 1])
                    pe.wait_ge(pb_copied, u + 1)
                else:
                    keys = [NL, NL + 1]
                pe.wait_ge(pa_copied, u + 1)
                if h % HQ == 0 and hh >= 2:
                    pe.wait_ge(o_ready, hh - 1)
                product(ps[6 + hh % 2][:, (h % HQ) * P:(h % HQ + 1) * P],
                        lambda b: probT[:, u % 2, b * P:(b + 1) * P],
                        lambda b: V[:, keys[b], (h // 8) * P:(h // 8 + 1) * P], len(keys)).then_inc(pv_done, 1)

            for u in range(U + 2):
                if u < U:
                    scores(u)
                if 1 <= u <= U:
                    turn_probs(u - 1)
                if u >= 2:
                    values(u - 2)
            barrier(pe)
            out_project(0, o_tok, oT, NT, J_WO0, None)
            n0 = experts(0, J_M0, None)
            extra = n0 * 16 - 16
            def low_rank():
                pe.wait_ge(small_loaded, SMALL["gla"])
                for b, c0, c1_ in ((0, 0, SEQ), (1, SEQ, SEQ + CTX)):
                    product(ps[b][0:2 * RANK, 0:c1_ - c0], lambda k: wa1[:, k, :], lambda k: hT[:, k, c0:c1_]).then_inc(a_product, 1)

            def gate_logits(n):
                t, d = divmod(n, 2)
                pe.wait_ge(a_copied, 2)
                pe.wait_ge(glaT_copied, min(n + 7, 8))
                if n >= 2:
                    pe.wait_ge(la_ready, n - 1)
                nc.tensor.matmul(ps[4 + n % 2][:], aT[:, t * P:(t + 1) * P], a2b[:, d, :],
                                 start=True, stop=True).then_inc(z_product, 1)

            def turn_gla(m):
                n, t = gla_steps[m]
                i = turn_of[m]
                pe.wait_ge(gla_evac, m + 1)
                if i >= 2:
                    pe.wait_ge(glaT_copied, i - 1)
                src = zq[:, m % 2] if n == 0 else ktok[:, t]
                for c in range(GH):
                    mm = nc.tensor.transpose(ps[4 + i % 2][:, c * P:(c + 1) * P], src[:, c * P:(c + 1) * P], ident)
                mm.then_inc(gla_turned, 1)

            NS = len(gla_steps)
            for step_ in range(NS + 1):
                if step_ < NT:
                    turn_tile("mix1", hbuf[:, step_ % 2], step_, normed)
                if step_ >= 1:
                    m = step_ - 1
                    n, t = gla_steps[m]
                    if t == 0:
                        wait_panel(pe, J_GLA + n, extra)
                    if n < 2:
                        pe.wait_ge(hT_copied, TURN["mix1"] + t + 1)
                    if m >= 2:
                        pe.wait_ge(gla_evac, m - 1)
                    product(ps[6 + m % 2][:], lambda k: hT[:, k, t * P:(t + 1) * P],
                            lambda k: panel(J_GLA + n)[:, k, :]).then_inc(gla_product, 1)
                    if m == Z0 - 1:
                        low_rank()
                    if Z0 <= m < Z0 + 2 * NT:
                        gate_logits(m - Z0)
                if step_ >= 3 and (step_ - 3) in turn_of:
                    turn_gla(step_ - 3)
            barrier(pe)
            barrier(pe)

            def sums(u):
                h, d = divmod(u, 2)
                cum, tail = (C("cum_f"), C("tail_f")) if d == 0 else (C("cum_b"), C("tail_b"))
                lac = lambda t: la[:, t, d, h * GK:(h + 1) * GK]
                if u >= 1:
                    pe.wait_ge(b_copied, u)
                    pe.wait_ge(tails_exp, u)
                for t in range(NL):
                    mm = nc.tensor.matmul(ps[0][:, t * P:(t + 1) * P], lac(t), cum, start=True, stop=True)
                mm.then_inc(b_done, 1)
                for t in range(NT):
                    bank = ps[1][:, t * P:(t + 1) * P] if t < 4 else ps[2][:, (t - 4) * P:(t - 3) * P]
                    nc.tensor.matmul(bank, tail, lac(t), start=True, stop=True)
                for t in range(NT):
                    mm = nc.tensor.matmul(ps[2][:, 256 + t:257 + t], lac(t), C("sixteenth"), start=True, stop=True)
                mm.then_inc(tails_done, 1)

            sums(0)
            for u in range(2 * GH):
                h, d = divmod(u, 2)
                if u + 1 < 2 * GH:
                    sums(u + 1)
                order = [4, 5, 0, 1, 2] if d == 0 else [5, 4, 3, 2, 1]
                pe.wait_ge(khat_ready, u + 1)
                for n, t in enumerate(order):
                    k = 5 * u + n
                    if k >= 2:
                        pe.wait_ge(state_ready, k - 1)
                    nc.tensor.matmul(ps[4 + k % 2][:, 0:GV], khat[d][:, t, :], Vg[:, t, h * GV:(h + 1) * GV],
                                     start=True, stop=True).then_inc(p_done, 1)
                    if n == 0:
                        continue
                    if n == 1:
                        pe.wait_ge(kq_ready, u + 1)
                        if u >= 1:
                            pe.wait_ge(s_masked, u)
                    for i in range(P // SUB):
                        c0 = (n - 1) * P + i * SUB
                        mm = nc.tensor.matmul(ps[3][:, c0:c0 + SUB], kp[d][:, n - 1, i, :], qp[d][:, c0:c0 + SUB],
                                              start=True, stop=True)
                mm.then_inc(s_done, 1)
                if d == 1:
                    pe.wait_ge(s_masked, u + 1)
                    pe.wait_ge(state_ready, 5 * (u + 1))
                    pe.wait_ge(qh_ready, h + 1)
                    for t in range(NL):
                        k = h * NL + t
                        if k >= 2:
                            pe.wait_ge(og_ready, k - 1)
                        o = ps[6 + k % 2][:, 0:GV]
                        v = Vg[:, t, h * GV:(h + 1) * GV]
                        for dd in range(2):
                            nc.tensor.matmul(o, qh[dd][:, t * P:(t + 1) * P], S[dd][:, t, :], start=(dd == 0), stop=False)
                            mm = nc.tensor.matmul(o, scT[dd][:, t, :], v, start=False, stop=(dd == 1))
                        mm.then_inc(og_done, 1)
            barrier(pe)
            out_project(1, G, oTg, NL, J_WO1, extra)
            experts(1, J_M1, extra)

        @block.scalar
        def _(act):
            step = Steps(act, act_steps)
            act.wait_ge(c_loaded, 16)
            act.wait_ge(consts_loaded, 16)
            nc.scalar.activation(csil, cT, ACT.Exp, scale=-1.0).then_inc(c_silu, 1)

            def square_tile(name, t):
                q = NORM[name][1] + t
                nc.scalar.activation(junks[name], X[:, t], ACT.Square, accum_out=ss[:, q:q + 1]).then_inc(sumsq_ready, 1)
                act.wait_ge(sumsq_ready, q + 1)

            def copy_turned(name, dst, t):
                g = TURN[name] + t
                act.wait_ge(h_turned, g + 1)
                step(nc.scalar.copy(dst[:, 0:4, t * P:(t + 1) * P], ps[2 * (g % 2)][:].rearrange("p (k n) -> p k n", k=4)))
                nc.scalar.copy(dst[:, 4:8, t * P:(t + 1) * P],
                               ps[2 * (g % 2) + 1][:].rearrange("p (k n) -> p k n", k=4)).then_inc(hT_copied, 1)

            def copy_turned_gla(m):
                n, t = gla_steps[m]
                i = turn_of[m]
                act.wait_ge(gla_turned, i + 1)
                dst = (qTg if n == 0 else kTg)[:, :, t * P:(t + 1) * P]
                nc.scalar.copy(dst, ps[4 + i % 2][:].rearrange("p (k n) -> p k n", k=4)).then_inc(glaT_copied, 1)

            def experts(l):
                s = L[l]
                T = NT if l == 0 else NL
                for t in range(T):
                    copy_turned(f"wo{l}", oT if l == 0 else oTg, t)
                for t in range(T + 1):
                    if t < T:
                        act.wait_ge(wo_added[l], 2 * (t + 1))
                        square_tile(f"ffn{l}", t)
                    if t >= 1:
                        copy_turned(f"ffn{l}", hT, t - 1)
                act.wait_ge(logits_done, l + 1)
                nc.scalar.activation(sc[:, 0:T].rearrange("p a b -> p (a b)"), ps[7][:, 0:T * NE], ACT.Exp, scale=-1.0).then_inc(gates_exp, 1)
                barrier(act)
                nblk = act.value_load(table_i[0:1, 31:32], min_val=NE, max_val=NE + MAX_EXTRA)

                def copy_xT():
                    return nc.scalar.copy(xT[:, 0:4, :], ps[0][:].rearrange("p (k n) -> p k n", k=4))

                act.wait_ge(s["x_turned"], 1)
                copy_xT().then_inc(s["xT_act"], 1)
                with act.Fori(0, nblk) as i:
                    act.wait_ge(s["gate_done"], i + 1)
                    nc.scalar.activation(sil, ps[2][:], ACT.Silu).then_inc(s["sil_ready"], 1)
                    act.wait_ge(s["x_turned"], i + 2)
                    copy_xT().then_inc(s["xT_act"], 1)
                    act.wait_ge(s["hid_turned"], i + 1)
                    nc.scalar.copy(hidT.rearrange("p f n -> p (f n)"), ps[4][:]).then_inc(s["hidT_ready"], 1)
                    act.wait_ge(s["down_done"], i + 1)
                    nc.scalar.copy(ysb[:, 0:512], ps[5][:]).then_inc(s["y0_ready"], 1)
                    act.wait_ge(s["y0_ready"], i + 1)
                    act.wait_ge(s["y1_ready"], i + 1)
                    act.dma_start(ybuf[bass.ds(i * P, P), :], ysb).then_inc(s["y_stored"], 16)
                    act.wait_ge(s["y_stored"], i * 16 + 16)
                barrier(act)
                nxt = "mix1" if l == 0 else "final"
                for t in range(T + 1):
                    if t < T:
                        act.wait_ge(combined, t + 1 + (0 if l == 0 else NT))
                        square_tile(nxt, t)
                    if l == 0 and t >= 1:
                        copy_turned("mix1", hT, t - 1)
                    if l == 0 and t >= 4:
                        copy_turned_gla(t - 4)

            def copy_ada(j):
                act.wait_ge(ada_partial, j + 1)
                if j >= 1:
                    act.wait_ge(mods_product, j)
                nc.scalar.copy(ada_sum, ps[4 + j % 2][:]).then_inc(ada_copied, 1)

            for j in range(ADA0):
                copy_ada(j)
                if j == ADA0 - 2:
                    act.wait_ge(x_in, 16 * NT)
                    for t in range(NT):
                        square_tile("mix0", t)
            barrier(act)
            for t in range(NT):
                copy_turned("mix0", hT, t)
            barrier(act)
            for m in range(3 * NT):
                n, t = divmod(m, NT)
                copy_ada(ADA0 + m)
                act.wait_ge(qkv_turned, m + 1)
                if n < 2:
                    ins = nc.scalar.copy(qT[:, 4 * n:4 * n + 4, t * P:(t + 1) * P], ps[2 + m % 2][:].rearrange("p (k n) -> p k n", k=4))
                else:
                    for par in range(2):
                        half = slice(64 * par, 64 * par + 64)
                        ins = nc.scalar.copy(kT[half, 2 * par:2 * par + 2, t * P:(t + 1) * P],
                                             ps[2 + m % 2][half, 0:256].rearrange("p (k n) -> p k n", k=2))
                        if par == 0:
                            step(ins)
                ins.then_inc(qkvT_copied, 1)
            barrier(act)

            U = NT * HEADS
            for u in range(U + 1):
                t, h = divmod(u, HEADS)
                if u < U:
                    st = att[:, (u // HQ) % 2]
                    hi = h % HQ
                    act.wait_ge(shift_ready, u + 1)
                    if u >= 2:
                        act.wait_ge(pa_turned, u - 1)
                    if hi == 0 and u >= 2 * HQ:
                        act.wait_ge(o_ready, u // HQ - 1)
                    na = 384 if t < NL else 256
                    a1 = nc.scalar.activation(prob[:, u % 2, 0:na], ps[u % 2][:, 0:na], ACT.Exp, bias=st[:, 8 + hi:9 + hi],
                                              scale=HD ** -0.5, accum_out=st[:, 16 + hi:17 + hi])
                    if t < NL:
                        step(a1)
                        nb = 256 if 0 < t < NL - 1 else 128
                        a1 = nc.scalar.activation(prob[:, u % 2, 384:384 + nb], prob[:, u % 2, 384:384 + nb], ACT.Exp,
                                                  bias=st[:, 8 + hi:9 + hi], scale=HD ** -0.5, accum_out=st[:, 24 + hi:25 + hi])
                    a1.then_inc(probs_ready, 1)
                if u >= 1:
                    v = u - 1
                    tv = v // HEADS
                    act.wait_ge(pa_turned, v + 1)
                    if v >= 2:
                        act.wait_ge(pv_done, v - 1)
                    na = 384 if tv < NL else 256
                    nc.scalar.copy(probT[:, v % 2, 0:na], ps[4][:, 0:na]).then_inc(pa_copied, 1)
                    if v % HQ == HQ - 1:
                        hh = v // HQ
                        sv = att[:, hh % 2]
                        act.wait_ge(sinkarg_ready, hh + 1)
                        nc.scalar.activation(sv[:, 32:32 + HQ], sv[:, 32:32 + HQ], ACT.Exp).then_inc(sinkexp_ready, 1)
            barrier(act)
            experts(0)
            def gate_logarithm(n):
                t, d = divmod(n, 2)
                l1 = la[:, t, d, :]
                act.wait_ge(z_product, n + 1)
                step(nc.scalar.activation(l1, ps[4 + n % 2][:], ACT.Abs))
                step(nc.scalar.activation(l1, l1, ACT.Exp, scale=-1.0))
                nc.scalar.activation(l1, l1, ACT.Ln, bias=C("one")).then_inc(ln_ready, 1)

            for m in range(len(gla_steps)):
                n, t = gla_steps[m]
                if m in turn_of and m > NT - 4:
                    copy_turned_gla(m)
                if m == Z0 - 1:
                    act.wait_ge(ones_row, 2)
                    for b, c0, c1_ in ((0, 0, SEQ), (1, SEQ, SEQ + CTX)):
                        act.wait_ge(a_product, b + 1)
                        nc.scalar.copy(aT[0:2 * RANK, c0:c1_], ps[b][0:2 * RANK, 0:c1_ - c0]).then_inc(a_copied, 1)
                if Z0 <= m < Z0 + 2 * NT:
                    gate_logarithm(m - Z0)
                if n >= 4:
                    act.wait_ge(gla_product, m + 1)
                    nc.scalar.activation(G[:, t, (n - 4) * 512:(n - 3) * 512], ps[6 + m % 2][:], ACT.Silu).then_inc(silu_g, 1)
            barrier(act)
            barrier(act)

            def exponentials(u):
                h, d = divmod(u, 2)
                act.wait_ge(b_done, u + 1)
                if u >= 2:
                    act.wait_ge(args_ready, u - 1)
                nc.scalar.copy(bT[d], ps[0][:]).then_inc(b_copied, 1)
                act.wait_ge(tails_done, u + 1)
                if u >= 2:
                    act.wait_ge(p_done, 5 * (u - 1))
                    act.wait_ge(state_ready, 5 * (u - 1))
                step(nc.scalar.activation(khat[d][:, 0:4, :].rearrange("p a b -> p (a b)"), ps[1][:], ACT.Exp))
                step(nc.scalar.activation(khat[d][:, 4:6, :].rearrange("p a b -> p (a b)"), ps[2][:, 0:256], ACT.Exp))
                nc.scalar.activation(dec[d][:, 0:NT], ps[2][:, 256:256 + NT], ACT.Exp).then_inc(tails_exp, 1)
                act.wait_ge(args_ready, u + 1)
                step(nc.scalar.activation(qp[d], qp[d], ACT.Exp))
                for i in range(4):
                    k0, k1 = (0, SUB * (i + 1)) if d == 0 else (SUB * i, P)
                    ins = nc.scalar.activation(kp[d][:, :, i, k0:k1], kp[d][:, :, i, k0:k1], ACT.Exp)
                    if i < 3:
                        step(ins)
                ins.then_inc(exps_ready, 1)
                if d == 1:
                    act.wait_ge(b_copied, u + 1)
                    if h >= 1:
                        act.wait_ge(og_done, NL * h)
                    step(nc.scalar.activation(qh[0], bT[0], ACT.Exp))
                    nc.scalar.activation(qh[1], bT[1], ACT.Exp).then_inc(qh_exp, 1)
                    act.wait_ge(qh_exp, h + 1)

            exponentials(0)
            for u in range(2 * GH):
                h, d = divmod(u, 2)
                if u + 1 < 2 * GH:
                    exponentials(u + 1)
                if d == 1:
                    for t in range(NL):
                        k = h * NL + t
                        act.wait_ge(og_done, k + 1)
                        if k >= 8:
                            act.wait_ge(og_ready, k - 7)
                        nc.scalar.activation(S[1][:, t, :], ps[6 + k % 2][:, 0:GV], ACT.Square, accum_out=ssg[:, k % 8:k % 8 + 1]).then_inc(og_sq, 1)
                        act.wait_ge(og_sq, k + 1)
            barrier(act)
            experts(1)

        @block.vector
        def _(dve):
            step = Steps(dve, dve_steps)
            dve.wait_ge(c_silu, 1)
            dve.wait_ge(consts_loaded, 16)
            step(nc.vector.tensor_scalar(csil, csil, 1.0, None, ALU.add))
            step(nc.vector.reciprocal(csil, csil))
            step(nc.vector.memset(c32, 0.0))
            nc.vector.tensor_tensor(csil, csil, cT, ALU.mult).then_inc(c_silu, 1)
            dve.wait_ge(c_silu, 2)
            nc.vector.tensor_copy(c32[:, :, 0:2], csil).then_inc(c_silu, 1)

            def add_bias(j):
                dve.wait_ge(mods_product, j + 1)
                if j < ADA0:
                    dve.wait_ge(first_loaded, 16)
                    cols = slice(j * PW, (j + 1) * PW)
                    nc.vector.tensor_tensor(first_out[0:2, cols], ps[6 + j % 2][0:2, :], first_bias[0:2, cols], ALU.add).then_inc(mods_added, 1)
                    return
                n = (j - ADA0) // 2
                dve.wait_ge(bias_loaded[j % 2], 16 * (n + 1))
                if n >= 1:
                    dve.wait_ge(mods_stored[j % 2], 16 * n)
                nc.vector.tensor_tensor(ada_out[0:2, j % 2], ps[6 + j % 2][0:2, :], ada_bias[0:2, j % 2], ALU.add).then_inc(mods_added, 1)

            for j in range(ADA0):
                add_bias(j)
            barrier(dve)
            rowcount = [0]

            def prepare_rows(name):
                rowcount[0] += 5
                dve.wait_ge(rows_loaded, 16 * rowcount[0])
                for stream in range(2):
                    step(nc.vector.scalar_tensor_tensor(out=rows[:, 2 * stream], in0=rows[:, 2 * stream], scalar=1.0,
                                                        in1=gain, op0=ALU.add, op1=ALU.mult))

            def norm_tile(name, t):
                q = NORM[name][1] + t
                st = 0 if t < NL else 1
                dve.wait_ge(rstd_ready, q + 1)
                if name == "final":
                    nc.vector.scalar_tensor_tensor(out=H[:, t], in0=X[:, t], scalar=rstd[:, q:q + 1], in1=rows[:, 0],
                                                   op0=ALU.mult, op1=ALU.mult).then_inc(normed, 1)
                    return
                h = H[:, t]
                if name.startswith("mix"):
                    h = hbuf[:, t % 2]
                    if t >= 2:
                        dve.wait_ge(h_turned, TURN[name] + t - 1)
                step(nc.vector.scalar_tensor_tensor(out=h, in0=X[:, t], scalar=rstd[:, q:q + 1], in1=rows[:, 2 * st],
                                                    op0=ALU.mult, op1=ALU.mult))
                nc.vector.tensor_tensor(h, h, rows[:, 2 * st + 1], ALU.add).then_inc(normed, 1)

            def out_project(l, T, grow, tmp):
                for t in range(T):
                    for n in range(2):
                        m = 2 * t + n
                        dve.wait_ge(wo_product[l], m + 1)
                        step(nc.vector.tensor_tensor(tmp, ps[4 + m % 3][:], grow(t)[:, n * 512:(n + 1) * 512], ALU.mult))
                        xs = X[:, t, n * 512:(n + 1) * 512]
                        nc.vector.tensor_tensor(xs, xs, tmp, ALU.add).then_inc(wo_added[l], 1)
                        dve.wait_ge(wo_added[l], m + 1)
                        if n == 0 and t >= 1:
                            norm_tile(f"ffn{l}", t - 1)
                    if t == 0:
                        prepare_rows(f"ffn{l}")
                norm_tile(f"ffn{l}", T - 1)

            def places(pos, s, g):
                for dl in (1, 2, 3):
                    step(nc.vector.tensor_tensor(g[:, :, 0:4 - dl], s[:, :, 0:4 - dl], s[:, :, dl:4], ALU.is_ge))
                    step(nc.vector.tensor_tensor(pos[:, :, dl:4], pos[:, :, dl:4], g[:, :, 0:4 - dl], ALU.add))
                    step(nc.vector.tensor_tensor(pos[:, :, 0:4 - dl], pos[:, :, 0:4 - dl], g[:, :, 0:4 - dl], ALU.subtract))

            def route(l):
                T = NT if l == 0 else NL
                tt, ts_ = nc.vector.tensor_tensor, nc.vector.tensor_scalar
                fl = lambda v: v[:, 0:T].rearrange("p a b -> p (a b)")
                gv = lambda v: fl(v).rearrange("p (g e) -> p g e", e=EPG)
                bc = lambda row: row.unsqueeze(1).to_broadcast([P, T, row.shape[1]])
                dve.wait_ge(gates_exp, l + 1)
                dve.wait_ge(small_loaded, SMALL["router"][l])
                step(ts_(fl(sc), fl(sc), 1.0, None, ALU.add))
                step(nc.vector.reciprocal(fl(sc), fl(sc)))
                step(tt(sel[:, 0:T], sc[:, 0:T], bc(rbrow), ALU.add))
                step(nc.vector.tensor_copy(posn[:, 0:T], bc(C("wins"))))
                places(gv(posn), gv(sel), gv(t96))
                step(ts_(fl(t96), fl(posn), 1.5, None, ALU.is_lt))
                step(tt(fl(t96b), fl(t96), fl(sel), ALU.mult))
                gflat = lambda v: v[:, 0:T].rearrange("p a b -> p (a b)")
                step(nc.vector.tensor_reduce(gflat(gs), gv(t96b), AX, ALU.add))
                step(nc.vector.tensor_copy(gpos[:, 0:T], bc(C("wins")[:, 0:NG])))
                places(gpos[:, 0:T], gs[:, 0:T], gt[:, 0:T])
                step(ts_(gflat(g1), gflat(gpos), 0.5, None, ALU.is_lt))
                g1b = gflat(g1).unsqueeze(2).to_broadcast([P, T * NG, EPG])
                step(ts_(fl(s1), fl(posn), 0.5, None, ALU.is_lt))
                step(tt(fl(s2), fl(t96), fl(s1), ALU.subtract))
                step(tt(gv(s1), gv(s1), g1b, ALU.mult))
                step(tt(gv(s2), gv(s2), g1b, ALU.mult))
                tt(fl(M), fl(s1), fl(s2), ALU.add).then_inc(picks_ready, 1)
                step(tt(fl(t96), fl(sc), fl(s1), ALU.mult))
                step(nc.vector.tensor_reduce(c1[:, 0:T], t96[:, 0:T], AX, ALU.add))
                step(tt(fl(t96), fl(sc), fl(s2), ALU.mult))
                step(nc.vector.tensor_reduce(c2[:, 0:T], t96[:, 0:T], AX, ALU.add))
                step(tt(gt_(T), c1[:, 0:T], c2[:, 0:T], ALU.add))
                step(nc.vector.reciprocal(gt_(T), gt_(T)))
                step(tt(c1[:, 0:T], c1[:, 0:T], gt_(T), ALU.mult))
                step(tt(c2[:, 0:T], c2[:, 0:T], gt_(T), ALU.mult))
                dve.wait_ge(ranks_done, l + 1)
                step(nc.vector.tensor_copy(cnt, ps[6][:, 0:NE]))
                step(ts_(ext, cnt, float(P) + 0.5, None, ALU.is_ge))
                for j in range(2, T):
                    step(nc.vector.scalar_tensor_tensor(out=ext, in0=cnt, scalar=float(P) * j + 0.5, in1=ext, op0=ALU.is_ge, op1=ALU.add))
                step(nc.vector.tensor_copy(incl, ext))
                x, y = incl, t16
                for dl in (1, 2, 4, 8):
                    step(nc.vector.tensor_copy(y[:, 0:dl], x[:, 0:dl]))
                    step(tt(y[:, dl:NE], x[:, dl:NE], x[:, 0:NE - dl], ALU.add))
                    x, y = y, x
                step(tt(ovb, x, ext, ALU.subtract))
                step(tt(big, incl.unsqueeze(1).to_broadcast([P, MAX_EXTRA, NE]),
                        C("idx")[:, 0:MAX_EXTRA].unsqueeze(2).to_broadcast([P, MAX_EXTRA, NE]), ALU.is_le))
                step(nc.vector.tensor_copy(tab[:, 0:NE], C("idx")))
                step(nc.vector.tensor_reduce(tab[:, NE:NE + MAX_EXTRA], big, AX, ALU.add))
                step(ts_(tab[:, NE:NE + MAX_EXTRA], tab[:, NE:NE + MAX_EXTRA], float(NE - 1), None, ALU.min))
                step(nc.vector.tensor_copy(tab[:, 28:31], C("idx")[:, 0:3]))
                step(ts_(tab[:, 31:32], incl[:, NE - 1:NE], float(NE), None, ALU.add))
                step(nc.vector.tensor_copy(table_i[:], tab))
                step(ts_(ovb, ovb, float(NE - 1), float(P), ALU.add, ALU.mult))
                step(tt(ovb, ovb, C("e128"), ALU.subtract))
                step(nc.vector.tensor_copy(fl(slot), ps[5][:, 0:T * NE]))
                step(ts_(fl(t96), fl(slot), float(P) - 0.5, None, ALU.is_ge))
                step(tt(t96[:, 0:T], t96[:, 0:T], bc(ovb), ALU.mult))
                step(tt(fl(slot), fl(slot), fl(t96), ALU.add))
                step(tt(slot[:, 0:T], slot[:, 0:T], bc(C("e128")), ALU.add))
                for c, s in enumerate((s1, s2)):
                    step(tt(fl(t96), fl(slot), fl(s), ALU.mult))
                    step(nc.vector.tensor_reduce(slotf[:, 0:T, c], t96[:, 0:T], AX, ALU.add))
                nc.vector.tensor_copy(slot_idx[:, 0:2 * T], slotf[:, 0:T].rearrange("p a b -> p (a b)")).then_inc(table_ready, 1)

            def gt_(T):
                return gt[:, 0:2].rearrange("p a b -> p (a b)")[:, 0:T]

            def leave_projection(m):
                n, t = gla_steps[m]
                z = ps[6 + m % 2][:]
                if n >= 4:
                    dve.wait_ge(small_loaded, SMALL["gla"])
                    dve.wait_ge(silu_g, m - gla_last[3] + 1)
                    g2 = G[:, t, (n - 4) * 512:(n - 3) * 512].rearrange("p (h v) -> p h v", h=2)
                    nc.vector.tensor_tensor(g2, g2, gnrow.unsqueeze(1).to_broadcast([P, 2, GV]), ALU.mult).then_inc(gla_evac, 1)
                    return
                dve.wait_ge(gla_product, m + 1)
                if n == 0:
                    if m >= 2:
                        dve.wait_ge(gla_turned, m - 1)
                    ins = nc.vector.tensor_scalar(zq[:, m % 2], z, GK ** -0.5, None, ALU.mult)
                elif n == 1:
                    ins = nc.vector.tensor_copy(ktok[:, t], z)
                else:
                    ins = nc.vector.tensor_copy(Vg[:, t, (n - 2) * 512:(n - 1) * 512], z)
                ins.then_inc(gla_evac, 1)

            def experts(l):
                s = L[l]
                T = NT if l == 0 else NL
                route(l)
                barrier(dve)
                nblk = dve.value_load(table_i[0:1, 31:32], min_val=NE, max_val=NE + MAX_EXTRA)

                def copy_xT():
                    return nc.vector.tensor_copy(xT[:, 4:8, :], ps[1][:].rearrange("p (k n) -> p k n", k=4))

                dve.wait_ge(s["x_turned"], 1)
                copy_xT().then_inc(s["xT_dve"], 1)
                with dve.Fori(0, nblk) as i:
                    dve.wait_ge(s["sil_ready"], i + 1)
                    dve.wait_ge(s["up_done"], i + 1)
                    nc.vector.tensor_tensor(hid, sil, ps[3][:], ALU.mult).then_inc(s["hid_ready"], 1)
                    dve.wait_ge(s["x_turned"], i + 2)
                    copy_xT().then_inc(s["xT_dve"], 1)
                    dve.wait_ge(s["down_done"], i + 1)
                    nc.vector.tensor_copy(ysb[:, 512:1024], ps[6][:]).then_inc(s["y1_ready"], 1)
                barrier(dve)
                dve.wait_ge(gates_loaded, 32 * (l + 2))
                if l == 0:
                    prepare_rows("mix1")
                else:
                    dve.wait_ge(rows_loaded, 16 * (rowcount[0] + 1))
                for t in range(T + 1):
                    if t < T:
                        m = t + (0 if l == 0 else NT)
                        base = 0 if l == 0 else 3 * 32
                        dve.wait_ge(gathered[t % 2], base + 32 * (t // 2 + 1))
                        ya, yb = comb[:, 2 * (t % 2)], comb[:, 2 * (t % 2) + 1]
                        grow = rows[:, 4 if t < NL else 5]
                        step(nc.vector.tensor_scalar(ya, ya, c1[:, t:t + 1], None, ALU.mult))
                        step(nc.vector.scalar_tensor_tensor(out=ya, in0=yb, scalar=c2[:, t:t + 1], in1=ya, op0=ALU.mult, op1=ALU.add))
                        step(nc.vector.tensor_tensor(ya, ya, grow, ALU.mult))
                        nc.vector.tensor_tensor(X[:, t], X[:, t], ya, ALU.add).then_inc(combined, 1)
                        dve.wait_ge(combined, m + 1)
                    if t >= 1:
                        norm_tile("mix1" if l == 0 else "final", t - 1)
                    if l == 0 and t >= 3:
                        leave_projection(t - 3)

            dve.wait_ge(x_in, 16 * NT)
            prepare_rows("mix0")
            for t in range(NT):
                norm_tile("mix0", t)
            barrier(dve)
            for m in range(3 * NT):
                n, t = divmod(m, NT)
                z = ps[m % 2]
                nh = 8 if n < 2 else 4
                w = nh * HD
                dve.wait_ge(qkv_product, m + 1)
                if m >= 2:
                    dve.wait_ge(qkv_turned, m - 1)
                dst = zb[:, m % 2]
                hv = lambda v: v[:, 0:w].rearrange("p (h d) -> p h d", h=nh)
                pv = (lambda v: v[:, 0:w].rearrange("p (a c d) -> p a c d", a=2, c=4)) if n < 2 else (lambda v: hv(v))
                dv = (lambda v: v[:, 0:w].rearrange("p (c a d) -> p a c d", a=2, c=4)) if n < 2 else (lambda v: hv(v))
                if n == 2:
                    step(nc.vector.tensor_copy(V[:, t, :], z[:, 256:512]))
                if t < NL:
                    cos, sin = C("cos")[:, t * HD:(t + 1) * HD], C("sin")[:, t * HD:(t + 1) * HD]
                    step(nc.vector.tensor_tensor(hv(rope_a), hv(z[:]), cos.unsqueeze(1).to_broadcast([P, nh, HD]), ALU.mult))
                    q4 = lambda v: v[:, 0:w].rearrange("p (h a f d) -> p h a f d", h=nh, a=2, f=2)
                    s4 = sin.rearrange("p (a f d) -> p a f d", a=2, f=2)
                    for f in range(2):
                        for ax in range(2):
                            step(nc.vector.tensor_tensor(q4(rope_b)[:, :, ax, f, :], q4(z[:])[:, :, ax, 1 - f, :],
                                                         s4[:, ax, f, :].unsqueeze(1).to_broadcast([P, nh, 16]), ALU.mult))
                    nc.vector.tensor_tensor(dv(dst), pv(rope_a), pv(rope_b), ALU.add).then_inc(z_ready, 1)
                else:
                    nc.vector.tensor_copy(dv(dst), pv(z[:])).then_inc(z_ready, 1)
                dve.wait_ge(z_ready, m + 1)
                add_bias(ADA0 + m)
            dve.wait_ge(small_loaded, SMALL["sinks"])
            step(nc.vector.tensor_scalar(sinkrow[:, HEADS:2 * HEADS], sinkrow[:, 0:HEADS], -1.0, None, ALU.mult))
            barrier(dve)

            U = NT * HEADS
            for u in range(U + 2):
                t, h = divmod(u, HEADS)
                if u < U:
                    st, hi = att[:, (u // HQ) % 2], h % HQ
                    dve.wait_ge(scores_done, u + 1)
                    na = 384 if t < NL else 256
                    if hi == 0 and u >= 2 * HQ:
                        dve.wait_ge(o_ready, u // HQ - 1)
                    step(nc.vector.tensor_reduce(st[:, hi:hi + 1], ps[u % 2][:, 0:na], AX, ALU.max))
                    top = st[:, hi:hi + 1]
                    if t < NL:
                        nb = 256 if 0 < t < NL - 1 else 128
                        win = C("win")[:, 0:256] if nb == 256 else (C("win")[:, 128:256] if t == 0 else C("win")[:, 0:128])
                        if u >= 2:
                            dve.wait_ge(pb_turned, u - 1)
                        step(nc.vector.tensor_tensor_reduce(out=prob[:, u % 2, 384:384 + nb], in0=ps[2 + u % 2][:, 0:nb], in1=win,
                                                            scale=1.0, scalar=top, op0=ALU.add, op1=ALU.max,
                                                            accum_out=st[:, 40 + hi:41 + hi]))
                        top = st[:, 40 + hi:41 + hi]
                    nc.vector.tensor_scalar(st[:, 8 + hi:9 + hi], top, -(HD ** -0.5), sinkrow[:, HEADS + h:HEADS + h + 1],
                                            ALU.mult, ALU.min).then_inc(shift_ready, 1)
                    dve.wait_ge(shift_ready, u + 1)
                    if hi == HQ - 1:
                        nc.vector.tensor_tensor(st[:, 32:32 + HQ], st[:, 8:8 + HQ], sinkrow[:, h - hi:h + 1], ALU.add).then_inc(sinkarg_ready, 1)
                if 1 <= u <= U and (u - 1) // HEADS < NL:
                    v = u - 1
                    tv = v // HEADS
                    nb = 256 if 0 < tv < NL - 1 else 128
                    dve.wait_ge(pb_turned, v + 1)
                    if v >= 2:
                        dve.wait_ge(pv_done, v - 1)
                    nc.vector.tensor_copy(probT[:, v % 2, 384:384 + nb], ps[5][:, 0:nb]).then_inc(pb_copied, 1)
                if u >= 2 and (u - 2) % HQ == HQ - 1:
                    hh = (u - 2) // HQ
                    tv, gq = divmod(hh, HEADS // HQ)
                    sv = att[:, hh % 2]
                    den = sv[:, 32:32 + HQ]
                    dve.wait_ge(probs_ready, HQ * (hh + 1))
                    dve.wait_ge(sinkexp_ready, hh + 1)
                    step(nc.vector.tensor_tensor(den, den, sv[:, 16:16 + HQ], ALU.add))
                    if tv < NL:
                        step(nc.vector.tensor_tensor(den, den, sv[:, 24:24 + HQ], ALU.add))
                    step(nc.vector.reciprocal(sv[:, 48:48 + HQ], den))
                    dve.wait_ge(pv_done, HQ * (hh + 1))
                    half = HD * (gq % 2)
                    nc.vector.tensor_tensor(o_tok[:, tv, gq * 256:(gq + 1) * 256].rearrange("p (h d) -> p h d", h=HQ),
                                            ps[6 + hh % 2][:].rearrange("p (h d) -> p h d", h=HQ)[:, :, half:half + HD],
                                            sv[:, 48:48 + HQ].unsqueeze(2).to_broadcast([P, HQ, HD]), ALU.mult).then_inc(o_ready, 1)
            barrier(dve)
            dve.wait_ge(gates_loaded, 32)
            out_project(0, NT, lambda t: rows[:, 4 if t < NL else 5], wo_tmp)
            experts(0)
            nc.vector.memset(aT, 0.0).then_inc(ones_row, 1)
            dve.wait_ge(ones_row, 1)
            nc.vector.memset(aT[2 * RANK:2 * RANK + 1], 1.0).then_inc(ones_row, 1)

            def gate_ready(n):
                t, d = divmod(n, 2)
                l1 = la[:, t, d, :]
                dve.wait_ge(ln_ready, n + 1)
                nc.vector.scalar_tensor_tensor(out=l1, in0=ps[4 + n % 2][:], scalar=0.0, in1=l1, op0=ALU.min,
                                               op1=ALU.subtract).then_inc(la_ready, 1)

            for m in range(NT - 2, len(gla_steps)):
                leave_projection(m)
                if Z0 <= m < Z0 + 2 * NT:
                    gate_ready(m - Z0)
            dve.wait_ge(la_ready, 2 * NT)
            barrier(dve)
            barrier(dve)
            spans = lambda d: [(i, 0, SUB * (i + 1)) if d == 0 else (i, SUB * i, P) for i in range(4)]

            def arguments(u):
                d = u % 2
                dve.wait_ge(b_copied, u + 1)
                if u >= 2:
                    dve.wait_ge(s_done, u - 1)
                subs = bT[d].rearrange("p (n w) -> p n w", w=SUB)
                refs = subs[:, :, SUB // 2]
                refs4 = refs.rearrange("p (t i) -> p t i", t=NL)
                b4 = bT[d].rearrange("p (t s) -> p t s", t=NL)
                step(nc.vector.tensor_tensor(qp[d].rearrange("p (n w) -> p n w", w=SUB), subs,
                                             refs.unsqueeze(2).to_broadcast([P, NL * 4, SUB]), ALU.subtract))
                for i, k0, k1 in spans(d):
                    ins = nc.vector.tensor_tensor(kp[d][:, :, i, k0:k1], refs4[:, :, i:i + 1].to_broadcast([P, NL, k1 - k0]),
                                                  b4[:, :, k0:k1], ALU.subtract)
                    if i < 3:
                        step(ins)
                ins.then_inc(args_ready, 1)

            def with_keys_and_queries(u):
                h, d = divmod(u, 2)
                dve.wait_ge(tails_exp, u + 1)
                nc.vector.tensor_tensor(khat[d], khat[d], ktok[:, :, h * GK:(h + 1) * GK], ALU.mult).then_inc(khat_ready, 1)
                dve.wait_ge(exps_ready, u + 1)
                step(nc.vector.tensor_tensor(qp[d], qp[d], qTg[:, h], ALU.mult))
                kh = kTg[:, h].rearrange("p (t s) -> p t s", t=NL)
                for i, k0, k1 in spans(d):
                    ins = nc.vector.tensor_tensor(kp[d][:, :, i, k0:k1], kp[d][:, :, i, k0:k1], kh[:, :, k0:k1], ALU.mult)
                    if i < 3:
                        step(ins)
                ins.then_inc(kq_ready, 1)

            arguments(0)
            with_keys_and_queries(0)
            for u in range(2 * GH):
                h, d = divmod(u, 2)
                if u + 1 < 2 * GH:
                    arguments(u + 1)
                order = [4, 5, 0, 1, 2] if d == 0 else [5, 4, 3, 2, 1]
                into = [None, 0, 1, 2, 3] if d == 0 else [None, 3, 2, 1, 0]
                for n, t in enumerate(order):
                    k = 5 * u + n
                    dst = S_tmp if n == 0 else S[d][:, into[n], :]
                    dve.wait_ge(p_done, k + 1)
                    if n == 0:
                        ins = nc.vector.tensor_copy(dst, ps[4 + k % 2][:, 0:GV])
                    else:
                        prev = S_tmp if n == 1 else S[d][:, into[n - 1], :]
                        ins = nc.vector.scalar_tensor_tensor(out=dst, in0=prev, scalar=dec[d][:, t:t + 1], in1=ps[4 + k % 2][:, 0:GV],
                                                             op0=ALU.mult, op1=ALU.add)
                    ins.then_inc(state_ready, 1)
                    dve.wait_ge(state_ready, k + 1)
                if u + 1 < 2 * GH:
                    with_keys_and_queries(u + 1)
                dve.wait_ge(s_done, u + 1)
                mask = C("mask_f") if d == 0 else C("mask_b")
                nc.vector.tensor_tensor(scT[d], ps[3][:].rearrange("p (t s) -> p t s", t=NL),
                                        mask.unsqueeze(1).to_broadcast([P, NL, P]), ALU.mult).then_inc(s_masked, 1)
                if d == 0:
                    dve.wait_ge(qh_exp, h + 1)
                    step(nc.vector.tensor_tensor(qh[0], qh[0], qTg[:, h], ALU.mult))
                    nc.vector.tensor_tensor(qh[1], qh[1], qTg[:, h], ALU.mult).then_inc(qh_ready, 1)
                else:
                    for t in range(NL):
                        k = h * NL + t
                        dve.wait_ge(og_rstd, k + 1)
                        g = G[:, t, h * GV:(h + 1) * GV]
                        nc.vector.scalar_tensor_tensor(out=g, in0=ps[6 + k % 2][:, 0:GV], scalar=rsg[:, k % 8:k % 8 + 1], in1=g,
                                                       op0=ALU.mult, op1=ALU.mult).then_inc(og_ready, 1)
            barrier(dve)
            dve.wait_ge(grow_loaded, 16)
            out_project(1, NL, lambda t: grow1, wo_tmp1)
            experts(1)


_INS = ["x", "ctx", "ada_w", "ada_b", "norm_mix_g", "norm_ffn_g", "final_g", "attn_w_qkv", "attn_w_o", "attn_sinks",
        "gla_w_in", "gla_norm_g", "gla_w_o", "router_w", "router_b", "moe_w_gate", "moe_w_up", "moe_w_down"]


def kernel(**inputs):
    import concourse.bacc as bacc
    from concourse.bass_utils import run_bass_kernel_spmd as run

    nc = bacc.Bacc("TRN2", target_bir_lowering=False, num_devices=1)
    arrays = {k: np.ascontiguousarray(inputs[k]) for k in _INS}
    both = np.stack([np.asarray(inputs["c"])[0], np.asarray(inputs["c_ctx"])])
    arrays["cT"] = np.ascontiguousarray(both.reshape(2, KC, P).transpose(2, 1, 0))
    arrays["wa1"] = np.ascontiguousarray(np.asarray(inputs["gla_w_a1"])[0].reshape(2, KC, P, RANK).transpose(2, 1, 0, 3).reshape(P, KC, 2 * RANK))
    a2b = np.zeros((P, 2, 512), np.float32)
    for d in range(2):
        a2b[d * RANK:(d + 1) * RANK, d] = np.asarray(inputs["gla_w_a2"])[0, d]
        a2b[2 * RANK, d] = np.asarray(inputs["gla_b_a"])[0, d]
    arrays["a2b"] = a2b
    arrays["const"] = constants()[0]
    aps = {k: nc.dram_tensor(f"in_{k}", v.shape, F32, kind="ExternalInput").ap() for k, v in arrays.items()}
    out = nc.dram_tensor("out", (SEQ, D), F32, kind="ExternalOutput").ap()
    build(nc, aps, out)
    r = run(nc, [{f"in_{k}": v for k, v in arrays.items()}], core_ids=[0])
    return np.asarray(r.results[0]["out"]).reshape(1, SEQ, D)
```
